# Optimizing a Trainium2 kernel written in Bass

```python
import jax, jax.numpy as jnp
from jax import lax
import numpy as np

D_MODEL = 1024
BATCH = 1
SEQ = 256
DEPTH = 2

GRID_W = 64
CTX_LEN = 256
RET_HEADS = 4
RET_QK_HEAD = 128
RET_V_HEAD = 256
RET_QK_WIDTH = RET_HEADS * RET_QK_HEAD
RET_V_WIDTH = RET_HEADS * RET_V_HEAD
CONV_WIDTH = 1024
CONV_TAPS = 3
D_FF = 2816
CHUNK = 128
N_MOD = 9
ROPE_BASE = 10000.0
NORM_EPS = 1e-6
IN_SECTIONS = (RET_QK_WIDTH, RET_V_WIDTH, RET_QK_WIDTH, RET_V_WIDTH, CONV_WIDTH, CONV_WIDTH, CONV_WIDTH, D_MODEL, D_MODEL)
IN_WIDTH = 2 * RET_QK_WIDTH + 2 * RET_V_WIDTH + 3 * CONV_WIDTH + 2 * D_MODEL
KV_WIDTH = RET_QK_WIDTH + RET_V_WIDTH

kernel_name = "hybrid_retention_shortconv_macaron_dit"

def rmsnorm(h, w):
    hf = h.astype(jnp.float32)
    hf = hf * lax.rsqrt(jnp.mean(hf * hf, axis=-1, keepdims=True) + NORM_EPS)
    return (hf * w.astype(jnp.float32)).astype(h.dtype)

def head_rmsnorm(o):
    return o * lax.rsqrt(jnp.mean(o * o, axis=-1, keepdims=True) + NORM_EPS)

def adaln_params(cond, w_mod, b_mod):
    m = jax.nn.silu(cond) @ w_mod + b_mod
    return m.reshape(cond.shape[0], 1, N_MOD, D_MODEL)

def modulated_norm(h, w, mod, i):
    return rmsnorm(h, w) * (1.0 + mod[:, :, 3 * i + 1]) + mod[:, :, 3 * i]

def swiglu(y, w_up, w_down):
    a, b = jnp.split(y @ w_up, 2, axis=-1)
    return (jax.nn.silu(a) * b) @ w_down

def ffn_sublayer(h, mod, i, norm_w, w_up, w_down):
    y = modulated_norm(h, norm_w, mod, i)
    return h + 0.5 * mod[:, :, 3 * i + 2] * swiglu(y, w_up, w_down)

def split_projection(p):
    pieces = []
    start = 0
    for width in IN_SECTIONS:
        pieces.append(p[..., start:start + width])
        start += width
    return pieces

def to_heads(t):
    b, n, w = t.shape
    return t.reshape(b, n, RET_HEADS, w // RET_HEADS).transpose(0, 2, 1, 3)

def axial_rope(t, pos_row, pos_col):
    half = t.shape[-1] // 2
    n_freq = half // 2
    inv_freq = ROPE_BASE ** (-jnp.arange(n_freq, dtype=jnp.float32) / n_freq)

    def rotate(part, pos):
        ang = pos.astype(jnp.float32)[:, None] * inv_freq[None, :]
        cos, sin = jnp.cos(ang).astype(t.dtype), jnp.sin(ang).astype(t.dtype)
        a, b = part[..., :n_freq], part[..., n_freq:]
        return jnp.concatenate([a * cos - b * sin, a * sin + b * cos], axis=-1)

    return jnp.concatenate([rotate(t[..., :half], pos_row), rotate(t[..., half:], pos_col)], axis=-1)

def retention_chunked(q, k, v, log_gamma, s0):
    batch, heads, n, dk = q.shape
    dv = v.shape[-1]
    nc = n // CHUNK
    qf = q.astype(jnp.float32).reshape(batch, heads, nc, CHUNK, dk)
    kf = k.astype(jnp.float32).reshape(batch, heads, nc, CHUNK, dk)
    vf = v.astype(jnp.float32).reshape(batch, heads, nc, CHUNK, dv)
    lg = log_gamma.astype(jnp.float32)[:, None]
    idx = jnp.arange(CHUNK, dtype=jnp.float32)
    rel = idx[:, None] - idx[None, :]
    intra_decay = jnp.where(rel >= 0, jnp.exp(lg[:, :, None] * jnp.maximum(rel, 0.0)), 0.0)
    scores = jnp.einsum('bhnid,bhnjd->bhnij', qf, kf) * intra_decay[None, :, None]
    intra = jnp.einsum('bhnij,bhnje->bhnie', scores, vf)
    k_weight = jnp.exp(lg * (CHUNK - 1 - idx))
    chunk_kv = jnp.einsum('bhnjd,bhnje->bhnde', kf * k_weight[None, :, None, :, None], vf)
    chunk_decay = jnp.exp(lg[:, 0] * CHUNK)[None, :, None, None]

    def step(state, kv_c):
        return chunk_decay * state + kv_c, state

    _, prev_states = lax.scan(step, s0, jnp.moveaxis(chunk_kv, 2, 0))
    q_weight = jnp.exp(lg * (idx + 1.0))
    cross = jnp.einsum('bhnid,nbhde->bhnie', qf * q_weight[None, :, None, :, None], prev_states)
    return (intra + cross).reshape(batch, heads, n, dv)

def bidir_retention(q, k, v, log_decay, s0_f, s0_b):
    flip = lambda t: jnp.flip(t, axis=2)
    fwd = retention_chunked(q, k, v, log_decay[0], s0_f)
    bwd = retention_chunked(flip(q), flip(k), flip(v), log_decay[1], s0_b)
    return fwd + flip(bwd)

def context_states(k, v, log_decay):
    length = k.shape[2]
    pos = jnp.arange(length, dtype=jnp.float32)
    lg = log_decay.astype(jnp.float32)
    w_f = jnp.exp(lg[0][:, None] * (length - 1 - pos))
    w_b = jnp.exp(lg[1][:, None] * pos)
    kf, vf = k.astype(jnp.float32), v.astype(jnp.float32)
    s_f = jnp.einsum('bhld,bhle->bhde', kf * w_f[None, :, :, None], vf)
    s_b = jnp.einsum('bhld,bhle->bhde', kf * w_b[None, :, :, None], vf)
    return s_f, s_b

def short_conv(u, w):
    up = jnp.pad(u, ((0, 0), (1, 1), (0, 0)))
    return w[0] * up[:, :-2] + w[1] * up[:, 1:-1] + w[2] * up[:, 2:]

def mixer_merge(o_ret, g, conv_b, conv_c, conv_x, gate_ret, gate_conv, conv_w, w_ret_out, w_conv_out, w_out):
    b, h, n, dv = o_ret.shape
    o = head_rmsnorm(o_ret).transpose(0, 2, 1, 3).reshape(b, n, h * dv).astype(g.dtype)
    y_ret = (jax.nn.silu(g) * o) @ w_ret_out
    y_conv = (conv_b * short_conv(conv_c * conv_x, conv_w)) @ w_conv_out
    merged = jax.nn.sigmoid(gate_ret) * y_ret + jax.nn.sigmoid(gate_conv) * y_conv
    return merged @ w_out

def setup_inputs(seed: int = 0) -> dict:
    key = jax.random.key(seed)
    ks = jax.random.split(key, 20)

    def nrm(k, shape, scale=1.0):
        return jax.random.normal(k, shape, jnp.float32) * scale

    base_decay = jnp.log1p(-jnp.power(2.0, -5.0 - jnp.arange(RET_HEADS, dtype=jnp.float32)))
    return {
        "x": nrm(ks[0], (BATCH, SEQ, D_MODEL)),
        "c": nrm(ks[1], (BATCH, D_MODEL)),
        "ctx": nrm(ks[2], (BATCH, CTX_LEN, D_MODEL)),
        "c_ctx": nrm(ks[3], (D_MODEL,)),
        "norm_w": 1.0 + nrm(ks[4], (DEPTH, 3, D_MODEL), 0.05),
        "w_mod": nrm(ks[5], (DEPTH, D_MODEL, N_MOD * D_MODEL), 0.3 * D_MODEL ** -0.5),
        "b_mod": nrm(ks[6], (DEPTH, N_MOD * D_MODEL), 0.02),
        "ffn1_w_up": nrm(ks[7], (DEPTH, D_MODEL, 2 * D_FF), D_MODEL ** -0.5),
        "ffn1_w_down": nrm(ks[8], (DEPTH, D_FF, D_MODEL), D_FF ** -0.5),
        "w_in": nrm(ks[9], (DEPTH, D_MODEL, IN_WIDTH), D_MODEL ** -0.5),
        "ret_log_decay": base_decay[None, None, :] * (1.0 + nrm(ks[10], (DEPTH, 2, RET_HEADS), 0.05)),
        "conv_w": nrm(ks[11], (DEPTH, CONV_TAPS, CONV_WIDTH), CONV_TAPS ** -0.5),
        "w_ret_out": nrm(ks[12], (DEPTH, RET_V_WIDTH, D_MODEL), RET_V_WIDTH ** -0.5),
        "w_conv_out": nrm(ks[13], (DEPTH, CONV_WIDTH, D_MODEL), CONV_WIDTH ** -0.5),
        "w_out": nrm(ks[14], (DEPTH, D_MODEL, D_MODEL), D_MODEL ** -0.5),
        "ffn2_w_up": nrm(ks[15], (DEPTH, D_MODEL, 2 * D_FF), D_MODEL ** -0.5),
        "ffn2_w_down": nrm(ks[16], (DEPTH, D_FF, D_MODEL), D_FF ** -0.5),
        "final_norm_w": 1.0 + nrm(ks[17], (D_MODEL,), 0.05),
    }

def reference(x, c, ctx, c_ctx, norm_w, w_mod, b_mod, ffn1_w_up, ffn1_w_down, w_in, ret_log_decay,
              conv_w, w_ret_out, w_conv_out, w_out, ffn2_w_up, ffn2_w_down, final_norm_w):
    batch, n_lat, _ = x.shape
    ROWS = n_lat // GRID_W
    pos_row = jnp.repeat(jnp.arange(ROWS), GRID_W)
    pos_col = jnp.tile(jnp.arange(GRID_W), ROWS)
    zero_state = jnp.zeros((batch, RET_HEADS, RET_QK_HEAD, RET_V_HEAD), jnp.float32)
    k_scale = RET_QK_HEAD ** -0.5

    for l in range(DEPTH):
        last = l == DEPTH - 1
        mod_x = adaln_params(c, w_mod[l], b_mod[l])
        mod_c = adaln_params(c_ctx[None], w_mod[l], b_mod[l])

        x = ffn_sublayer(x, mod_x, 0, norm_w[l, 0], ffn1_w_up[l], ffn1_w_down[l])
        ctx = ffn_sublayer(ctx, mod_c, 0, norm_w[l, 0], ffn1_w_up[l], ffn1_w_down[l])

        yx = modulated_norm(x, norm_w[l, 1], mod_x, 1)
        yc = modulated_norm(ctx, norm_w[l, 1], mod_c, 1)
        px = split_projection(yx @ w_in[l])
        if last:
            kc_raw, vc_raw = jnp.split(yc @ w_in[l][:, :KV_WIDTH], [RET_QK_WIDTH], axis=-1)
        else:
            pc = split_projection(yc @ w_in[l])
            kc_raw, vc_raw = pc[0], pc[1]
        kc = to_heads(kc_raw) * k_scale
        vc = to_heads(vc_raw)
        s_f, s_b = context_states(kc, vc, ret_log_decay[l])

        kx = axial_rope(to_heads(px[0]) * k_scale, pos_row, pos_col)
        vx = to_heads(px[1])
        qx = axial_rope(to_heads(px[2]), pos_row, pos_col)
        o_x = bidir_retention(qx, kx, vx, ret_log_decay[l], s_f, s_b)
        x = x + mod_x[:, :, 5] * mixer_merge(o_x, *px[3:], conv_w[l], w_ret_out[l], w_conv_out[l], w_out[l])
        if not last:
            qc = to_heads(pc[2])
            o_c = bidir_retention(qc, kc, vc, ret_log_decay[l], zero_state, zero_state)
            ctx = ctx + mod_c[:, :, 5] * mixer_merge(o_c, *pc[3:], conv_w[l], w_ret_out[l], w_conv_out[l], w_out[l])

        x = ffn_sublayer(x, mod_x, 2, norm_w[l, 2], ffn2_w_up[l], ffn2_w_down[l])
        if not last:
            ctx = ffn_sublayer(ctx, mod_c, 2, norm_w[l, 2], ffn2_w_up[l], ffn2_w_down[l])

    return rmsnorm(x, final_norm_w)


_drawn_inputs = setup_inputs


def setup_inputs(seed=0):
    import zlib

    import numpy as np

    out = dict(_drawn_inputs(seed))
    spreads = {}
    factors = {'c_ctx': 3.007, 'norm_w': 2.982}
    for name, (base, spread) in spreads.items():
        noise = np.random.default_rng([zlib.crc32(name.encode()), seed]).standard_normal(out[name].shape)
        drawn = base * np.exp(spread * noise) if base else spread * noise
        out[name] = __import__('jax').numpy.asarray(drawn.astype(out[name].dtype))
    for name, factor in factors.items():
        out[name] = (out[name] * factor).astype(out[name].dtype)
    return out
```

```python
import math
from contextlib import ExitStack

import numpy as np
import concourse.bass as bass
from concourse import mybir

F32 = mybir.dt.float32
F32R = mybir.dt.float32r
ACT = mybir.ActivationFunctionType
ALU = mybir.AluOpType
AXX = mybir.AxisListType.X

P = 128
D = 1024
KT = D // P
NX = 256
NC = 256
DEPTH = 2
HEADS, DK, DV = 4, 128, 256
FF = 2816
JF = FF // P
EPS = 1e-6
GRID_W = 64
ROPE_BASE = 10000.0
UW = 1024
RAW_SLOTS, HL_SLOTS = 4, 2
SECTIONS = 9
COL_K, COL_V, COL_Q, COL_G, COL_CB, COL_CC, COL_CX, COL_GR, COL_GC = (
    0, 512, 1536, 2048, 3072, 4096, 5120, 6144, 7168)
VT_BMOD = (0, 128)
VT_NORM, VT_C, VT_CONV, VT_CCTX, VT_FINAL = 72, 120, 200, 248, 256
CK_ID, CK_QS = 0, 128
CM_COS, CM_SIN, CM_SWAP, CM_REL, CM_RELP, CM_RELN, CM_CF, CM_CB = (
    0, 256, 512, 640, 1152, 1664, 2176, 2688)
CM_W = 3200


def constants():
    p = np.arange(P)
    keep = np.zeros((P, 256), np.float32)
    keep[p, CK_ID + p] = 1.0
    keep[:, CK_QS:CK_QS + P] = (p[:, None] % 32 == p[None, :] % 32)
    mix = np.zeros((P, CM_W), np.float32)
    tok = np.arange(NX)
    n_freq = DK // 4
    inv = (np.float32(ROPE_BASE) ** (-np.arange(n_freq, dtype=np.float32) / np.float32(n_freq))).astype(np.float32)
    pos = np.stack([tok // GRID_W, tok % GRID_W]).astype(np.float32)
    ang = pos[p // 64][:, :] * inv[p % 32][:, None]
    sign = np.where((p // 32) % 2 == 0, -1.0, 1.0).astype(np.float32)[:, None]
    mix[:, CM_COS:CM_COS + NX] = np.cos(ang)
    mix[:, CM_SIN:CM_SIN + NX] = np.sin(ang) * sign
    mix[p, CM_SWAP + (p ^ 32)] = 1.0
    key = (np.arange(2)[None, :, None] * P + p[:, None, None]).astype(np.float32)
    q = tok[None, None, :].astype(np.float32)
    rel = (q - key).reshape(P, 512)
    mix[:, CM_REL:CM_REL + 512] = rel
    mix[:, CM_RELP:CM_RELP + 512] = np.maximum(rel, 0)
    mix[:, CM_RELN:CM_RELN + 512] = np.maximum(-rel, 0)
    mix[:, CM_CF:CM_CF + 512] = (q + NC - key).reshape(P, 512)
    mix[:, CM_CB:CM_CB + 512] = (NX - q + key).reshape(P, 512)
    return keep, mix


class Stage:

    def __init__(self, kind, layer, T, n, at, entry, which=0, mods=None, last=False):
        self.kind, self.layer, self.T, self.n, self.entry = kind, layer, T, n, entry
        self.which, self.mods, self.last = which, mods, last
        self.u, self.o, self.h = at["u"], at["o"], at["h"]
        self.first, self.half, self.merged = at["first"], at["half"], at["merged"]
        self.mix, self.sq, self.evac = at["mix"], at["sq"], at["evac"]
        self.sec, self.ss, self.y = at["sec"], at["ss"], at["y"]
        self.score, self.ov, self.on, self.rot = at["score"], at["ov"], at["on"], at["rot"]
        self.hpart = at["hpart"]


COUNTERS = ("u", "o", "first", "half", "merged", "mix", "h", "sq", "evac", "sec", "ss", "y",
            "score", "ov", "on", "rot", "hpart")


def plan():
    at = {name: 0 for name in COUNTERS}
    at["sec"] = 2
    at["h"] = KT
    at["sq"] = KT + 1
    stages, free = [], []

    def add(kind, layer, T, n, adds, frees, **kw):
        nonlocal free
        s = Stage(kind, layer, T, n, at, list(free), **kw)
        for k, v in adds.items():
            at[k] += v
        free = [(f, at[f]) for f in frees]
        stages.append(s)

    for layer in range(DEPTH):
        last = layer == DEPTH - 1
        T2 = NX if last else NX + NC

        def ffn(which, T, mods):
            mods_up = 5 if mods is not None else 0
            small = T == NX
            add("up", layer, T, JF, dict(u=2 * JF, o=JF, first=JF, ss=1, y=KT, sec=mods_up,
                                         **({"half": 2 * JF, "merged": 2 * JF} if small else {})),
                ["merged"] if small else ["first", "o"], which=which, mods=mods)
            add("down", layer, T, KT, dict(u=3 * KT, h=KT, hpart=KT, sq=KT + 1, sec=2 if mods is not None else 0),
                ["h"], which=which, mods=mods, last=last and which == 1)

        ffn(0, NX + NC, 0 if not last else None)
        small = T2 == NX
        add("k", layer, NX + NC, 4, dict(u=4, evac=4, ss=1, y=KT), ["evac"])
        if small:
            add("q", layer, T2, 4, dict(u=4, half=4, merged=4), ["merged"])
        else:
            add("q", layer, T2, 4, dict(u=4, evac=4), ["evac"])
        add("v", layer, NX + NC, 8, dict(u=8, evac=8, rot=4), ["evac"])
        nP, nO = (2, 1) if small else (3, 2)
        add("ret", layer, T2, HEADS,
            dict(mix=nP * HEADS, score=nP * HEADS, ov=nO * HEADS, evac=nO * HEADS, ss=HEADS, on=2 * HEADS),
            ["mix", "evac"])
        hm = lambda k: {"half": k, "merged": k} if small else {}
        add("g", layer, T2, KT, dict(u=8, o=8, first=8, **hm(8)), ["merged"] if small else ["first"])
        add("conv", layer, T2, KT, dict(u=24, o=8, mix=32, sec=0 if last else 2,
                                        **({} if small else {"first": 8}), **hm(24)),
            ["merged"] if small else ["first", "mix", "o"], mods=None if last else 1)
        add("gates", layer, T2, KT, dict(u=32, o=8, first=16, mix=16, **hm(32)),
            ["merged"] if small else ["first", "mix"])
        add("out", layer, T2, KT, dict(u=8, h=KT, hpart=KT, sq=KT + 1), ["h"])
        ffn(1, T2, 1 if not last else None)
    add("final", DEPTH - 1, NX, 0, dict(ss=1), [])
    return stages, at


def build(nc, x, c, ctx_in, c_ctx, norm_w, w_mod, b_mod, up1, down1, w_in, log_decay, conv_w,
          w_ret, w_conv, w_out, up2, down2, final_w, keep_in, mix_in, out):
    stages, totals = plan()
    es = ExitStack()
    cursor = [16512]

    def place(name, shape, dt=F32, at=None):
        size = 4 * int(np.prod(shape[1:]))
        if at is None:
            at = cursor[0]
            cursor[0] += (size + 31) // 32 * 32
        return nc.alloc_sbuf_tensor_at(name, shape, dt, offset=at)

    H = place("H", [P, KT, 512])
    Y = place("Y", [P, KT, 2, 512], F32R)
    zone = cursor[0]
    cursor[0] += 98304
    Z = place("Z", [P, JF, 2, 512], F32R, zone)
    R = place("R", [P, KT, 2, 512], F32R, zone)
    CM = place("CM", [P, CM_W], F32, zone)
    G4 = place("G4", [P, 4, 512], F32, zone + 4 * CM_W)
    PX = place("PX", [P, 2, 4, 256], F32, zone + 4 * CM_W)
    PC = place("PC", [P, 2, 2, 256], F32, zone + 4 * CM_W + 8192)
    C = place("C", [P, KT, 2, 512], F32R, zone + 32768)
    DEC = place("DEC", [P, HEADS, 4, 256], F32, zone + 32768)
    O = place("O", [P, KT, 512], F32, zone + 32768 + 16384)
    KTT = place("KTT", [P, HEADS, 512], F32, zone + 65536)
    QTT = place("QTT", [P, HEADS, 512], F32, zone + 65536 + 8192)
    V = place("V", [P, 4, HEADS * DV], F32, zone + 65536 + 16384)
    M = place("M", [P, KT, 2, 512], F32R, zone + 65536)
    MODRAW = [place(f"MODRAW{s}", [P, UW], F32, zone + 90112 + 4096 * s) for s in range(2)]
    XROWS = place("XROWS", [P, 4, D], F32, zone)
    VROWS = place("VROWS", [P, 3, P], F32, zone + 16384)
    OROWS = place("OROWS", [P, 2, D], F32, zone)
    RAW = [place(f"RAW{s}", [P, UW]) for s in range(RAW_SLOTS)]
    HI = [place(f"HI{s}", [P, UW], F32R) for s in range(HL_SLOTS)]
    LO = [place(f"LO{s}", [P, UW], F32R) for s in range(HL_SLOTS)]
    TMP = place("TMP", [P, 4, 512])
    SQACC = place("SQACC", [P, 512])
    RB = place("RB", [P, 512])
    CV = place("CV", [P, 512])
    U = place("U", [P, 2, 258])
    MODACC = place("MODACC", [P, 2, UW])
    HB = place("HB", [P, 4, 256], F32, cursor[0] - 8192)
    MT = place("MT", [P, 512])
    MR = place("MR", [P, 64])
    CK = place("CK", [P, 256])
    ONES = place("ONES", [P, P])
    VT = place("VT", [P, 264])
    MODS = place("MODS", [P, DEPTH * SECTIONS, 2, KT])
    AMUL = place("AMUL", [P, 2, KT])
    GATE = place("GATE", [P, 2, KT])
    SC = place("SC", [P, 2, KT])
    LG = place("LG", [P, DEPTH * 2 * HEADS])
    EPST = place("EPST", [P, 1])
    assert cursor[0] <= nc.sbuf_usable_end, cursor[0]

    with es:
        B = [es.enter_context(nc.psum_tensor(f"bank{i}", [P, 512], F32)) for i in range(8)]
        names = {}

        def sem(name):
            names[name] = es.enter_context(nc.semaphore(name))
            return names[name]

        raw_landed = [sem(f"raw_landed{s}") for s in range(RAW_SLOTS)]
        mod_landed = [sem(f"mod_landed{s}") for s in range(2)]
        vec_landed, const_landed, x_landed, mixc_landed = (
            sem("vec_landed"), sem("const_landed"), sem("x_landed"), sem("mixc_landed"))
        hi_done, lo_done, unit_done = sem("hi_done"), sem("lo_done"), sem("unit_done")
        first_done, prod_done, ophi_done, oplo_done = (
            sem("first_done"), sem("prod_done"), sem("ophi_done"), sem("oplo_done"))
        half_done, merged_done, mix_done = sem("half_done"), sem("merged_done"), sem("mix_done")
        h_done, sq_done, sqsum_done = sem("h_done"), sem("sq_done"), sem("sqsum_done")
        ss_done, rt_done, rb_done = sem("ss_done"), sem("rt_done"), sem("rb_done")
        y_scaled, y_done, yhi_done, ylo_done = (
            sem("y_scaled"), sem("y_done"), sem("yhi_done"), sem("ylo_done"))
        evac_done, rot_done, rope_part, rope_done = (
            sem("evac_done"), sem("rot_done"), sem("rope_part"), sem("rope_done"))
        exp_done, dec_part, dec_done = sem("exp_done"), sem("dec_part"), sem("dec_done")
        score_done, ov_done, osq_done, osum_done, on_done = (
            sem("score_done"), sem("ov_done"), sem("osq_done"), sem("osum_done"), sem("on_done"))
        mod_step, mod_fin, mod_sum, mods_ready, amul_done = (
            sem("mod_step"), sem("mod_fin"), sem("mod_sum"), sem("mods_ready"), sem("amul_done"))
        small_set, vec_turned, vt_done, sc_done, x_turned = (
            sem("small_set"), sem("vec_turned"), sem("vt_done"), sem("sc_done"), sem("x_turned"))
        out_turned, out_copied, out_stored = sem("out_turned"), sem("out_copied"), sem("out_stored")
        block = es.enter_context(nc.Block())
        FREES = {"first": first_done, "o": prod_done, "merged": merged_done, "h": h_done,
                 "evac": evac_done, "mix": mix_done}

        start = [0]

        def at(i, rate, base):
            if isinstance(i, int):
                return base + rate * i
            return i * rate + (base - rate * start[0])

        def raw_wait(eng, u, per, i):
            eng.wait_ge(raw_landed[u % RAW_SLOTS], at(i, 16 * per // RAW_SLOTS, 16 * (u // RAW_SLOTS + 1)))

        def loops(s):
            if s.kind == "up":
                parts = [(None, 0, 2, False), (5, 2, 4, s.mods is not None)]
            elif s.kind == "down":
                if s.last:
                    parts = [(None, 0, 4, False), (None, 4, 4, False)]
                else:
                    parts = [(2, 0, 4, s.mods is not None)]
            elif s.kind == "conv":
                parts = [(2, 0, 4, s.mods is not None)]
            elif s.kind == "g" or s.kind == "out":
                parts = [(2, 0, 4, False)]
            elif s.kind == "gates":
                parts = [(4, 0, 2, False)]
            elif s.kind in ("k", "q"):
                parts = [(None, 0, 4, False)]
            else:
                raise ValueError(s.kind)
            return parts

        PER_TILE = {"up": 2, "down": 3, "conv": 3, "g": 1, "out": 1, "gates": 4, "k": 1, "q": 1}
        BANK = 4

        def run(eng, s, body):
            for count, t0, tiles, mods in loops(s):
                per = tiles * PER_TILE[s.kind]
                u0 = s.u + t0 * PER_TILE[s.kind]
                if count is None:
                    body(0, t0, tiles, mods, u0, per)
                else:
                    first = 1 if eng is nc.sync and s.kind != "up" else 0
                    start[0] = first
                    with eng.Fori(first, first + count) as i:
                        body(i, t0, tiles, mods, u0, per)
                    start[0] = 0

        def unit_words(s, c):
            return (JF - 2 * KT) * P if s.kind == "down" and c % 3 == 2 else UW

        last_u = totals["u"]
        UP, DOWN = (up1, up2), (down1, down2)

        @block.sync
        def _(sp):
            def mod_piece(sec_static, rate, i, k):
                if 2 * (8 * sec_static + k - 1) > 0:
                    sp.wait_ge(mod_step, at(i, 16 * rate, 2 * (8 * sec_static + k - 1)))
                layer, sec = sec_static // SECTIONS, sec_static % SECTIONS
                col = at(i, UW, sec * UW) if rate else sec * UW
                sp.dma_start(MODRAW[k % 2][:], w_mod[layer][k * P:(k + 1) * P, bass.ds(col, UW)]
                             ).then_inc(mod_landed[k % 2], 16)

            def load(u, per, i, src, words=UW):
                if u - RAW_SLOTS + 1 > 0:
                    sp.wait_ge(lo_done, at(i, per, u - RAW_SLOTS + 1))
                dst = RAW[u % RAW_SLOTS][:, 0:words]
                shape = dict(k=src.shape[1])
                sp.dma_start(dst.rearrange("p (k n) -> p k n", **shape), src
                             ).then_inc(raw_landed[u % RAW_SLOTS], 16)

            def block_of(w, k0, nk, col):
                v = w.rearrange("(k p) n -> p k n", p=P)
                return v[:, k0:k0 + nk, bass.ds(col, P)]

            row = 0
            for g, parts in enumerate((
                    ((b_mod[0], 0), (norm_w.rearrange("l i d -> (l i d)"), 72), (c[0], 120)),
                    ((b_mod[1], 0), (conv_w.rearrange("l i d -> (l i d)"), 72), (c_ctx, 120)),
                    ((final_w, 0),))):
                for src, r in parts:
                    rows = src.rearrange("(r p) -> r p", p=P)
                    sp.dma_start(VROWS[r:r + rows.shape[0], g, :], rows).then_inc(vec_landed, 16)
            sp.dma_start(CK[:], keep_in).then_inc(const_landed, 16)
            lg = log_decay.rearrange("l d h -> (l d h)")
            sp.dma_start(LG[:], lg.partition_broadcast(P)).then_inc(const_landed, 16)
            for k in range(2):
                mod_piece(0, 0, 0, k)
            for t, src in enumerate((x[0], ctx_in[0])):
                sp.dma_start(XROWS[:, 2 * t:2 * t + 2, :], src.rearrange("(t p) d -> p t d", p=P)
                             ).then_inc(x_landed, 16)
            for k in range(2, 8):
                mod_piece(0, 0, 0, k)
            for k in range(8):
                mod_piece(1, 0, 0, k)

            for s in stages:
                if s.kind == "up":
                    w = UP[s.which][s.layer]
                    if s.mods is not None:
                        if s.u > 0:
                            sp.wait_ge(unit_done, s.u)

                    def body(i, t0, tiles, mods, u0, per):
                        for cc in range(per):
                            col = at(i, tiles * P, (t0 + cc // 2) * P + (cc % 2) * FF)
                            load(u0 + cc, per, i, block_of(w, 0, KT, col))
                            if mods:
                                mod_piece(s.sec, 1, i, cc)
                    run(sp, s, body)
                elif s.kind == "down":
                    w = DOWN[s.which][s.layer]

                    def body(i, t0, tiles, mods, u0, per):
                        for cc in range(per):
                            k0 = KT * (cc % 3)
                            load(u0 + cc, per, i, block_of(w, k0, min(KT, JF - k0), at(i, tiles * P, (t0 + cc // 3) * P)),
                                 unit_words(s, cc))
                            if mods and cc < 8:
                                mod_piece(s.sec, 1, i, cc)
                    run(sp, s, body)
                elif s.kind in ("k", "q", "g", "out", "conv", "gates"):
                    wl = w_in[s.layer]
                    if s.kind == "conv" and s.mods is not None:
                        sp.wait_ge(ov_done, s.ov)
                    parts = {"k": [(wl, COL_K)], "q": [(wl, COL_Q)], "g": [(wl, COL_G)],
                             "conv": [(wl, COL_CC), (wl, COL_CX), (wl, COL_CB)],
                             "gates": [(wl, COL_GR), (wl, COL_GC), (w_ret[s.layer], 0), (w_conv[s.layer], 0)],
                             "out": [(w_out[s.layer], 0)]}[s.kind]

                    def body(i, t0, tiles, mods, u0, per):
                        for cc in range(per):
                            w, base = parts[cc % len(parts)]
                            load(u0 + cc, per, i, block_of(w, 0, KT, at(i, tiles * P, base + (cc // len(parts)) * P)))
                            if mods and cc < 8:
                                mod_piece(s.sec, 1, i, cc)
                    run(sp, s, body)
                elif s.kind == "v":
                    v = w_in[s.layer].rearrange("(k p) n -> p k n", p=P)
                    for cc in range(8):
                        half, kp = cc // 4, cc % 4
                        load(s.u + cc, 0, 0, v[:, 2 * kp:2 * kp + 2, COL_V + 512 * half:COL_V + 512 * half + 512])
                elif s.kind == "final":
                    sp.wait_ge(out_copied, 4)
                    sp.dma_start(out[0].rearrange("(t p) d -> p t d", p=P), OROWS[:]).then_inc(out_stored, 16)
                    sp.wait_ge(out_stored, 16)

        @block.tensor
        def _(pe):
            mm = nc.tensor.matmul

            def block_mm(bank, slot, kk, X, k, T, first, last):
                hi, lo = HI[slot][:, kk * P:(kk + 1) * P], LO[slot][:, kk * P:(kk + 1) * P]
                if T == 512:
                    mm(bank[:], hi, X[:, k, 0, :], start=first, stop=False)
                    mm(bank[:], hi, X[:, k, 1, :], start=False, stop=False)
                    return mm(bank[:], lo, X[:, k, 0, :], start=False, stop=last)
                mm(bank[:], hi, X[:, k, :, 0:NX], start=first, stop=False)
                return mm(bank[:, 0:NX], lo, X[:, k, 0, 0:NX], start=False, stop=last)

            def unit(u, per, i, bank, X, k0, nk, T, first=True, last=True):
                slot = u % HL_SLOTS
                pe.wait_ge(lo_done, at(i, per, u + 1))
                for kk in range(nk):
                    ins = block_mm(bank, slot, kk, X, k0 + kk, T, first and kk == 0, last and kk == nk - 1)
                ins.then_inc(unit_done, 1)

            def first_two(s):
                pe.wait_ge(lo_done, s.u + 2)
                for k in range(KT):
                    pe.wait_ge(ylo_done, s.y + k + 1)
                    for uu in range(2):
                        ins = block_mm(B[uu], (s.u + uu) % HL_SLOTS, k, Y, k, s.T, k == 0, k == KT - 1)
                        if k == KT - 1:
                            ins.then_inc(unit_done, 1)

            def sumsq(s):
                pe.wait_ge(sqsum_done, s.sq)
                mm(B[4][:, 0:s.T], ONES[:], SQACC[:, 0:s.T], start=True, stop=True).then_inc(ss_done, 1)

            def mod_total(sec, rate, i):
                pe.wait_ge(mod_fin, at(i, 8 * rate, 8 * (sec + 1)))
                mm(B[5][:, 0:64], CK[:, CK_QS:CK_QS + P], MR[:], start=True, stop=True).then_inc(mod_sum, 1)

            pe.wait_ge(vec_landed, 16 * 7)
            pe.wait_ge(const_landed, 32)
            pe.wait_ge(small_set, 2)
            ident = CK[:, CK_ID:CK_ID + P]
            for g in range(3):
                n = P if g < 2 else KT
                nc.tensor.transpose(B[g][:, 0:n], VROWS[0:n, g, :], ident[0:n, 0:n]).then_inc(vec_turned, 1)
            pe.wait_ge(x_landed, 32)
            pe.wait_ge(vt_done, 3)
            for k in range(KT):
                for t in range(4):
                    ins = nc.tensor.transpose(B[k][:, t * P:(t + 1) * P], XROWS[:, t, k * P:(k + 1) * P], ident)
                ins.then_inc(x_turned, 1)
            pe.wait_ge(h_done, KT)
            for sec in range(2):
                mod_total(sec, 0, 0)

            for s in stages:
                for name, count in s.entry:
                    pe.wait_ge(FREES[name], count)
                small = s.T == NX
                if s.kind == "up":
                    sumsq(s)
                    first_two(s)

                    def body(i, t0, tiles, mods, u0, per):
                        for cc in range(per):
                            if t0 == 0 and cc < 2:
                                continue
                            j = t0 + cc // 2
                            if small:
                                pe.wait_ge(merged_done, at(i, per, s.merged + 2 * t0 + cc - BANK + 1))
                            elif cc % 2 == 0:
                                if s.first + j - 1 > 0:
                                    pe.wait_ge(first_done, at(i, tiles, s.first + j - 1))
                            else:
                                if s.o + j - 1 > 0:
                                    pe.wait_ge(prod_done, at(i, tiles, s.o + j - 1))
                            unit(u0 + cc, per, i, B[cc % BANK], Y, 0, KT, s.T)
                        if mods:
                            mod_total(s.sec, 1, i)
                    run(pe, s, body)
                elif s.kind == "down":
                    def body(i, t0, tiles, mods, u0, per):
                        for cc in range(per):
                            n, part = t0 + cc // 3, cc % 3
                            if part == 0:
                                pe.wait_ge(h_done, at(i, tiles, s.h + n - BANK + 1))
                            pe.wait_ge(oplo_done, s.o - JF + min(JF, KT * (part + 1)))
                            nk = min(KT, JF - KT * part)
                            unit(u0 + cc, per, i, B[n % BANK], Z, KT * part, nk, s.T, part == 0, part == 2)
                        if mods:
                            mod_total(s.sec, 1, i)
                    run(pe, s, body)
                elif s.kind == "k":
                    sumsq(s)
                    first_two(s)
                    for cc in (2, 3):
                        unit(s.u + cc, 0, 0, B[cc], Y, 0, KT, s.T)
                elif s.kind == "q":
                    for cc in range(4):
                        unit(s.u + cc, 0, 0, B[cc], Y, 0, KT, s.T)
                elif s.kind == "v":
                    def rots(first, src):
                        for g in range(2):
                            mm(B[4 + first + g][:], CM[:, CM_SWAP:CM_SWAP + P], src[:, 2 * g:2 * g + 2, 0:NX],
                               start=True, stop=True).then_inc(rot_done, 1)
                    pe.wait_ge(mixc_landed, 16 * (s.layer + 1))
                    rots(0, KTT)
                    if not small:
                        pass
                    for cc in range(8):
                        half, kp = cc // 4, cc % 4
                        u = s.u + cc
                        pe.wait_ge(lo_done, u + 1)
                        for kk in range(2):
                            k = 2 * kp + kk
                            for tt in range(4):
                                if half == 1 and k == 0:
                                    pe.wait_ge(evac_done, s.evac + tt + 1)
                                for a, w in ((0, HI), (0, LO), (1, HI)):
                                    ins = mm(B[tt][:], Y[:, k, a, tt * P:(tt + 1) * P],
                                             w[u % HL_SLOTS][:, kk * 512:(kk + 1) * 512],
                                             start=(k == 0 and (a, w) == (0, HI)), stop=(k == KT - 1 and a == 1))
                        ins.then_inc(unit_done, 1)
                        if cc == 0:
                            rots(2, QTT)
                elif s.kind == "ret":
                    nP, nO = (2, 1) if small else (3, 2)
                    pe.wait_ge(rope_done, 4 * (s.layer + 1))

                    def scores(h):
                        if h >= 2:
                            pe.wait_ge(mix_done, s.mix + nP * (h - 1))
                        for half in range(2):
                            bank = B[2 * (h % 2) + half]
                            for q in range(2):
                                j = 2 * half + q
                                ins = mm(bank[:, q * NX:(q + 1) * NX], KTT[:, h, j * P:(j + 1) * P], QTT[:, h, 0:NX],
                                         start=True, stop=True)
                            ins.then_inc(score_done, 1)
                        if not small:
                            if h:
                                pe.wait_ge(mix_done, s.mix + nP * h)
                            for q in range(2):
                                ins = mm(B[4][:, q * NX:(q + 1) * NX], KTT[:, h, NX + q * P:NX + (q + 1) * P],
                                         QTT[:, h, NX:NX + NC], start=True, stop=True)
                            ins.then_inc(score_done, 1)

                    def outputs(h):
                        pe.wait_ge(mix_done, s.mix + nP * (h + 1))
                        if h:
                            pe.wait_ge(evac_done, s.evac + nO * h)
                        for dv in range(2):
                            for j in range(4):
                                ins = mm(B[5][:, dv * NX:(dv + 1) * NX],
                                         V[:, j, h * DV + dv * P:h * DV + (dv + 1) * P], PX[:, h % 2, j, :],
                                         start=(j == 0), stop=(j == 3))
                        ins.then_inc(ov_done, 1)
                        if not small:
                            for dv in range(2):
                                for j in range(2):
                                    ins = mm(B[6][:, dv * NX:(dv + 1) * NX],
                                             V[:, 2 + j, h * DV + dv * P:h * DV + (dv + 1) * P], PC[:, h % 2, j, :],
                                             start=(j == 0), stop=(j == 1))
                            ins.then_inc(ov_done, 1)

                    def head_sumsq(h):
                        pe.wait_ge(osum_done, HEADS * s.layer + h + 1)
                        pe.wait_ge(rt_done, s.ss + h)
                        mm(B[7][:, 0:s.T], ONES[:], TMP[:, 2 * (h % 2), 0:s.T], start=True, stop=True
                           ).then_inc(ss_done, 1)

                    scores(0)
                    scores(1)
                    outputs(0)
                    scores(2)
                    outputs(1)
                    head_sumsq(0)
                    scores(3)
                    outputs(2)
                    head_sumsq(1)
                    outputs(3)
                    head_sumsq(2)
                    head_sumsq(3)
                elif s.kind == "g":
                    def body(i, t0, tiles, mods, u0, per):
                        for cc in range(per):
                            if small:
                                pe.wait_ge(merged_done, at(i, per, s.merged + cc - BANK + 1))
                            else:
                                pe.wait_ge(first_done, at(i, per, s.first + cc - BANK + 1))
                            unit(u0 + cc, per, i, B[cc % BANK], Y, 0, KT, s.T)
                    run(pe, s, body)
                elif s.kind == "conv":
                    def body(i, t0, tiles, mods, u0, per):
                        for cc in range(per):
                            n, role = (cc - BANK) // 3, (cc - BANK) % 3
                            if small:
                                pe.wait_ge(merged_done, at(i, per, s.merged + cc - BANK + 1))
                            elif role == 0:
                                pe.wait_ge(first_done, at(i, tiles, s.first + n + 1))
                            elif role == 1:
                                pe.wait_ge(mix_done, at(i, 4 * tiles, s.mix + 4 * n + 1))
                            else:
                                pe.wait_ge(prod_done, at(i, tiles, s.o + n + 1))
                            unit(u0 + cc, per, i, B[cc % BANK], Y, 0, KT, s.T)
                        if mods:
                            mod_total(s.sec, 1, i)
                    run(pe, s, body)
                elif s.kind == "gates":
                    pe.wait_ge(oplo_done, s.o)
                    src = (Y, Y, R, C)

                    def body(i, t0, tiles, mods, u0, per):
                        for cc in range(per):
                            n, role = cc // 4 - 1, cc % 4
                            if small:
                                pe.wait_ge(merged_done, at(i, per, s.merged + cc - BANK + 1))
                            elif role < 2:
                                pe.wait_ge(first_done, at(i, 2 * tiles, s.first + 2 * n + role + 1))
                            else:
                                pe.wait_ge(mix_done, at(i, 2 * tiles, s.mix + 2 * n + role - 1))
                            unit(u0 + cc, per, i, B[cc % BANK], src[role], 0, KT, s.T)
                    run(pe, s, body)
                elif s.kind == "out":
                    pe.wait_ge(oplo_done, s.o)

                    def body(i, t0, tiles, mods, u0, per):
                        for cc in range(per):
                            pe.wait_ge(h_done, at(i, per, s.h + cc - BANK + 1))
                            unit(u0 + cc, per, i, B[cc % BANK], M, 0, KT, s.T)
                    run(pe, s, body)
                else:
                    sumsq(s)
                    for k in range(KT):
                        pe.wait_ge(y_done, s.y + k + 1)
                        for t in range(2):
                            nc.tensor.transpose(B[2 * t + k // 4][:, (k % 4) * P:(k % 4 + 1) * P],
                                                TMP[:, k % 4, t * P:(t + 1) * P],
                                                ident).then_inc(out_turned, 1)

        @block.scalar
        def _(act):
            A = nc.scalar.activation

            def split_hi(u, per, i, words=UW):
                if u >= last_u and isinstance(i, int):
                    return
                raw_wait(act, u, per, i)
                if u - HL_SLOTS + 1 > 0:
                    act.wait_ge(unit_done, at(i, per, u - HL_SLOTS + 1))
                A(HI[u % HL_SLOTS][:, 0:words], RAW[u % RAW_SLOTS][:, 0:words], ACT.Copy).then_inc(hi_done, 1)

            def next_words(s, cc, per):
                return unit_words(s, cc + 1) if cc + 1 < per else UW

            def square(base_h, base_sq, n, rate, i, src_tile, T):
                act.wait_ge(h_done, at(i, rate, base_h + n + 1))
                if base_sq + n > 0:
                    act.wait_ge(sqsum_done, at(i, rate, base_sq + n))
                A(TMP[:, n % 2, 0:T], src_tile, ACT.Square).then_inc(sq_done, 1)

            def root(s_ss, n, T, ss_bank):
                act.wait_ge(ss_done, s_ss + 1)
                A(RB[:, 0:T], ss_bank[:, 0:T], ACT.Sqrt, bias=EPST[:, 0:1], scale=1.0 / n).then_inc(rt_done, 1)

            def y_hi(s):
                root(s.ss, D, s.T, B[4])
                for k in range(KT):
                    act.wait_ge(y_done, s.y + k + 1)
                    A(Y[:, k, 0, 0:s.T], TMP[:, k % 4, 0:s.T], ACT.Copy).then_inc(yhi_done, 1)

            def half_copy(s, u, per, i, c, rel, o_wait, o_rate):
                act.wait_ge(unit_done, at(i, per, u + 1))
                act.wait_ge(prod_done, at(i, o_rate, o_wait))
                A(HB[:, c % BANK, :], B[c % BANK][:, NX:2 * NX], ACT.Copy).then_inc(half_done, 1)

            def operand_hi(o, rate, i, dst, T):
                act.wait_ge(prod_done, at(i, rate, o + 1))
                A(dst, TMP[:, 2 + o % 2, 0:T], ACT.Copy).then_inc(ophi_done, 1)

            act.wait_ge(vt_done, 2)
            A(SC[:, 0, :], VT[:, VT_C:VT_C + KT], ACT.Silu)
            A(SC[:, 1, :], VT[:, VT_CCTX:VT_CCTX + KT], ACT.Silu).then_inc(sc_done, 1)
            for k in range(KT):
                square(0, 0, k, 0, 0, H[:, k, :], 512)
            split_hi(0, 0, 0)

            for s in stages:
                T, small = s.T, s.T == NX
                if s.kind == "up":
                    def body(i, t0, tiles, mods, u0, per):
                        for cc in range(per):
                            j, jj = t0 + cc // 2, cc // 2
                            split_hi(u0 + cc + 1, per, i)
                            if t0 == 0 and cc == 0:
                                y_hi(s)
                            if small:
                                half_copy(s, u0 + cc, per, i, cc, 0, s.o + j - 1, tiles)
                            if cc % 2 == 0:
                                if small:
                                    act.wait_ge(merged_done, at(i, per, s.merged + 2 * t0 + cc + 1))
                                    src = HB[:, cc % BANK, :]
                                else:
                                    act.wait_ge(unit_done, at(i, per, u0 + cc + 1))
                                    src = B[cc % BANK][:, 0:T]
                                if s.o + j - 1 > 0:
                                    act.wait_ge(prod_done, at(i, tiles, s.o + j - 1))
                                A(TMP[:, (s.o + j) % 2, 0:T], src, ACT.Silu).then_inc(first_done, 1)
                            else:
                                operand_hi(s.o + j, tiles, i, Z[:, bass.ds(i * tiles + j, 1), 0, 0:T], T)
                    run(act, s, body)
                elif s.kind == "down" or s.kind == "out":
                    def body(i, t0, tiles, mods, u0, per):
                        for cc in range(per):
                            split_hi(u0 + cc + 1, per, i, next_words(s, cc, per))
                            if cc % PER_TILE[s.kind] == PER_TILE[s.kind] - 1:
                                n = t0 + cc // PER_TILE[s.kind]
                                square(s.h, s.sq, n, tiles, i, H[:, bass.ds(i * tiles + n, 1), 0:T], T)
                    run(act, s, body)
                elif s.kind == "k" or s.kind == "q":
                    scale = DK ** -0.5 if s.kind == "k" else 1.0
                    dst = KTT if s.kind == "k" else QTT
                    for cc in range(4):
                        split_hi(s.u + cc + 1, 0, 0)
                        if s.kind == "k" and cc == 0:
                            y_hi(s)
                        if small:
                            half_copy(s, s.u + cc, 0, 0, cc, 0, s.o, 0)
                        else:
                            act.wait_ge(unit_done, s.u + cc + 1)
                            A(dst[:, cc, 0:T], B[cc][:, 0:T], ACT.Copy, scale=scale).then_inc(evac_done, 1)
                elif s.kind == "v":
                    act.wait_ge(mixc_landed, 16 * (s.layer + 1))
                    lgw = 2 * HEADS * s.layer
                    for cc in range(8):
                        split_hi(s.u + cc + 1, 0, 0)
                        if cc % 2 == 0:
                            h = cc // 2
                            f, b = LG[:, lgw + h:lgw + h + 1], LG[:, lgw + HEADS + h:lgw + HEADS + h + 1]
                            for n, (col, g) in enumerate(((CM_RELP, f), (CM_RELN, b), (CM_CF, f), (CM_CB, b))):
                                if h or s.layer:
                                    act.wait_ge(dec_done, 2 * (HEADS * s.layer + h) - (1 if n < 2 else 0))
                                A(G4[:, n, :], CM[:, col:col + 512], ACT.Exp, scale=g).then_inc(exp_done, 1)
                        if cc % 4 == 3:
                            act.wait_ge(unit_done, s.u + cc + 1)
                            for tt in range(4):
                                A(V[:, tt, (cc // 4) * 512:(cc // 4 + 1) * 512], B[tt][:], ACT.Copy
                                  ).then_inc(evac_done, 1)
                elif s.kind == "ret":
                    nO = 1 if small else 2

                    def head_out(h):
                        for e in range(nO):
                            act.wait_ge(ov_done, s.ov + nO * h + e + 1)
                            A(O[:, 2 * h:2 * h + 2, e * NX:(e + 1) * NX],
                              B[5 + e][:].rearrange("p (a b) -> p a b", a=2), ACT.Copy).then_inc(evac_done, 1)
                        act.wait_ge(evac_done, s.evac + nO * (h + 1))
                        if h >= 2:
                            act.wait_ge(ss_done, s.ss + h - 1)
                        A(TMP[:, 2 * (h % 2):2 * (h % 2) + 2, 0:T], O[:, 2 * h:2 * h + 2, 0:T], ACT.Square
                          ).then_inc(osq_done, 1)

                    def head_root(h):
                        if h:
                            act.wait_ge(on_done, s.on + 2 * h)
                        root(s.ss + h, DV, T, B[7])
                    head_out(0)
                    head_out(1)
                    head_root(0)
                    head_out(2)
                    head_root(1)
                    head_out(3)
                    head_root(2)
                    head_root(3)
                elif s.kind == "g":
                    def body(i, t0, tiles, mods, u0, per):
                        for cc in range(per):
                            split_hi(u0 + cc + 1, per, i)
                            if small:
                                half_copy(s, u0 + cc, per, i, cc, 0, s.o + cc - 1, per)
                                act.wait_ge(merged_done, at(i, per, s.merged + cc + 1))
                                src = HB[:, cc % BANK, :]
                            else:
                                act.wait_ge(unit_done, at(i, per, u0 + cc + 1))
                                src = B[cc % BANK][:, 0:T]
                            act.wait_ge(prod_done, at(i, per, s.o + cc - 1))
                            A(TMP[:, cc % 2, 0:T], src, ACT.Silu).then_inc(first_done, 1)
                            operand_hi(s.o + cc, per, i, R[:, bass.ds(i * per + cc, 1), 0, 0:T], T)
                    run(act, s, body)
                elif s.kind == "conv":
                    def body(i, t0, tiles, mods, u0, per):
                        for cc in range(per):
                            n, role = cc // 3, cc % 3
                            split_hi(u0 + cc + 1, per, i)
                            if small:
                                half_copy(s, u0 + cc, per, i, cc, 0, s.o + n, tiles)
                            elif role == 0:
                                act.wait_ge(unit_done, at(i, per, u0 + cc + 1))
                                act.wait_ge(prod_done, at(i, tiles, s.o + n - 1))
                                A(TMP[:, n % 2, 0:T], B[cc % BANK][:, 0:T], ACT.Copy).then_inc(first_done, 1)
                            if role == 2:
                                operand_hi(s.o + n, tiles, i, C[:, bass.ds(i * tiles + n, 1), 0, 0:T], T)
                    run(act, s, body)
                elif s.kind == "gates":
                    def body(i, t0, tiles, mods, u0, per):
                        for cc in range(per):
                            n, role = cc // 4, cc % 4
                            split_hi(u0 + cc + 1, per, i)
                            if small:
                                half_copy(s, u0 + cc, per, i, cc, 0, s.o + n, tiles)
                            if role < 2:
                                if small:
                                    act.wait_ge(merged_done, at(i, per, s.merged + cc + 1))
                                    src = HB[:, cc % BANK, :]
                                else:
                                    act.wait_ge(unit_done, at(i, per, u0 + cc + 1))
                                    src = B[cc % BANK][:, 0:T]
                                act.wait_ge(prod_done, at(i, tiles, s.o + n - (1 - role)))
                                dst = TMP[:, n % 2, 0:T] if role == 0 else CV[:, 0:T]
                                A(dst, src, ACT.Sigmoid).then_inc(first_done, 1)
                            if role == 3:
                                operand_hi(s.o + n, tiles, i, M[:, bass.ds(i * tiles + n, 1), 0, 0:T], T)
                    run(act, s, body)
                else:
                    root(s.ss, D, T, B[4])
                    for b in range(4):
                        act.wait_ge(out_turned, 8 + 8 * (b % 2))
                        t, kk = b // 2, b % 2
                        A(OROWS[:, t, kk * 512:(kk + 1) * 512], B[b][:], ACT.Copy).then_inc(out_copied, 1)

        @block.vector
        def _(dve):
            V_ = nc.vector

            def split_lo(u, per, i, words=UW):
                if u >= last_u and isinstance(i, int):
                    return
                dve.wait_ge(hi_done, at(i, per, u + 1))
                V_.tensor_tensor(LO[u % HL_SLOTS][:, 0:words], RAW[u % RAW_SLOTS][:, 0:words],
                                 HI[u % HL_SLOTS][:, 0:words].bitcast(F32), ALU.subtract).then_inc(lo_done, 1)

            def next_words(s, cc, per):
                return unit_words(s, cc + 1) if cc + 1 < per else UW

            def mod_piece(sec, rate, i, k):
                dve.wait_ge(mod_landed[k % 2], at(i, 64 * rate, 16 * (4 * sec + k // 2 + 1)))
                for cond in range(2):
                    acc, a = MODACC[:, cond, :], SC[:, cond, k:k + 1]
                    if k == 0:
                        V_.tensor_scalar(acc, MODRAW[0][:], a, None, ALU.mult).then_inc(mod_step, 1)
                    else:
                        dve.wait_ge(mod_step, at(i, 16 * rate, 16 * sec + 2 * k + cond - 1))
                        V_.scalar_tensor_tensor(acc, MODRAW[k % 2][:], a, acc, ALU.mult, ALU.add
                                                ).then_inc(mod_step, 1)

            def mod_reduce(sec, rate, i):
                dve.wait_ge(mod_step, at(i, 16 * rate, 16 * (sec + 1)))
                for r in range(4):
                    src = MODACC[:, r // 2, (r % 2) * 512:(r % 2 + 1) * 512]
                    if r:
                        dve.wait_ge(mod_fin, at(i, 8 * rate, 8 * sec + 2 * r))
                    V_.transpose(MT[:], src).then_inc(mod_fin, 1)
                    dve.wait_ge(mod_fin, at(i, 8 * rate, 8 * sec + 2 * r + 1))
                    V_.tensor_reduce(MR[:, 16 * r:16 * r + 16], MT[:].rearrange("p (b k) -> p b k", k=32),
                                     AXX, ALU.add).then_inc(mod_fin, 1)

            def mod_store(sec, rate, i):
                dve.wait_ge(mod_sum, at(i, rate, sec + 1))
                layer, within = sec // SECTIONS, sec % SECTIONS
                total = B[5][:, 0:64].rearrange("p (c m r) -> p c m r", c=2, r=4)
                for r in range(4):
                    rows = slice(32 * r, 32 * r + 32)
                    for cond in range(2):
                        dst = MODS[rows, bass.ds(i + sec, 1), cond, :] if rate else MODS[rows, sec, cond, :]
                        bias = (VT[rows, bass.ds(i * KT + VT_BMOD[layer] + within * KT, KT)] if rate else
                                VT[rows, VT_BMOD[layer] + within * KT:VT_BMOD[layer] + (within + 1) * KT])
                        V_.tensor_tensor(dst, total[rows, cond, :, r], bias, ALU.add).then_inc(mods_ready, 1)

            def add_square(base, n, rate, i, T):
                dve.wait_ge(sq_done, at(i, rate, base - base // (KT + 1) + n + 1))
                dve.wait_ge(sqsum_done, at(i, rate, base + n + 1))
                V_.tensor_tensor(SQACC[:, 0:T], SQACC[:, 0:T], TMP[:, n % 2, 0:T], ALU.add).then_inc(sqsum_done, 1)

            def clear_squares():
                V_.memset(SQACC[:], 0.0).then_inc(sqsum_done, 1)

            def section(layer, n):
                return MODS[:, SECTIONS * layer + n, :, :]

            norm_count = [0]

            def reciprocal(ss, T):
                dve.wait_ge(rt_done, ss + 1)
                V_.reciprocal(RB[:, 0:T], RB[:, 0:T]).then_inc(rb_done, 1)
                dve.wait_ge(rb_done, ss + 1)

            def norm(s, which):
                T, layer = s.T, s.layer
                dve.wait_ge(mods_ready, 8 * (SECTIONS * layer + 3 * which + 2))
                norm_count[0] += 1
                w = VT[:, VT_NORM + (3 * layer + which) * KT:VT_NORM + (3 * layer + which + 1) * KT]
                for cond in range(2):
                    V_.scalar_tensor_tensor(AMUL[:, cond, :], section(layer, 3 * which + 1)[:, cond, :], 1.0, w,
                                            ALU.add, ALU.mult).then_inc(amul_done, 1)
                dve.wait_ge(amul_done, 2 * norm_count[0])
                reciprocal(s.ss, T)

                def scaled(k):
                    if k >= 4:
                        dve.wait_ge(ylo_done, s.y + k - 3)
                    V_.tensor_tensor(TMP[:, k % 4, 0:T], H[:, k, 0:T], RB[:, 0:T], ALU.mult).then_inc(y_scaled, 1)
                scaled(0)
                for k in range(KT):
                    if k + 1 < KT:
                        scaled(k + 1)
                    dve.wait_ge(y_scaled, s.y + k + 1)
                    for cond in range(T // NX):
                        t = TMP[:, k % 4, cond * NX:(cond + 1) * NX]
                        ins = V_.tensor_scalar(t, t, AMUL[:, cond, k:k + 1],
                                               section(layer, 3 * which)[:, cond, k:k + 1], ALU.mult, ALU.add)
                    ins.then_inc(y_done, 1)

            gate_count = [0]
            gate_set = sem("gate_set")

            def set_gate(s, sec, factor):
                dve.wait_ge(mods_ready, 8 * (SECTIONS * s.layer + sec + 1))
                gate_count[0] += 1
                V_.tensor_scalar(GATE[:], section(s.layer, sec), factor, None, ALU.mult).then_inc(gate_set, 1)
                dve.wait_ge(gate_set, gate_count[0])

            def residual(s, u, per, n, rate, i):
                dve.wait_ge(unit_done, at(i, per, u + 1))
                T = s.T
                for part in range(2):
                    cond = part if T == 512 else 0
                    cols = slice(cond * NX, (cond + 1) * NX)
                    dst = H[:, bass.ds(i * rate + n, 1), cols].rearrange("p a n -> p (a n)")
                    g = GATE[:, cond, bass.ds(i * rate + n, 1)]
                    if T == NX and part == 1:
                        dve.wait_ge(hpart_done, at(i, rate, s.hpart + n + 1))
                    ins = V_.scalar_tensor_tensor(dst, B[n % BANK][:, part * NX:(part + 1) * NX], g, dst,
                                                  ALU.mult, ALU.add)
                    ins.then_inc(hpart_done if part == 0 else h_done, 1)
            hpart_done = sem("hpart_done")
            def merge(s, c, rel, per, i, dst=None):
                dve.wait_ge(half_done, at(i, per, s.half + rel + 1))
                hb = HB[:, c % BANK, :]
                V_.tensor_tensor(dst if dst is not None else hb, B[c % BANK][:, 0:NX], hb, ALU.add
                                 ).then_inc(merged_done, 1)

            V_.memset(ONES[:], 1.0).then_inc(small_set, 1)
            V_.memset(EPST[:], EPS).then_inc(small_set, 1)
            V_.memset(U[:], 0.0).then_inc(small_set, 1)
            clear_squares()
            for g in range(3):
                n = P if g < 2 else KT
                dve.wait_ge(vec_turned, g + 1)
                V_.tensor_copy(VT[:, g * P:g * P + n], B[g][:, 0:n]).then_inc(vt_done, 1)
            for k in range(KT):
                dve.wait_ge(x_turned, k + 1)
                V_.tensor_copy(H[:, k, :], B[k][:]).then_inc(h_done, 1)
                if k:
                    add_square(0, k - 1, 0, 0, 512)
            add_square(0, KT - 1, 0, 0, 512)
            dve.wait_ge(sc_done, 1)
            dve.wait_ge(vt_done, 3)
            for sec in range(2):
                for k in range(8):
                    mod_piece(sec, 0, 0, k)
                mod_reduce(sec, 0, 0)
                mod_store(sec, 0, 0)
            split_lo(0, 0, 0)

            for s in stages:
                T, small = s.T, s.T == NX
                if s.kind == "up":
                    def body(i, t0, tiles, mods, u0, per):
                        for cc in range(per):
                            j, jj = t0 + cc // 2, cc // 2
                            o = s.o + j
                            split_lo(u0 + cc + 1, per, i)
                            if t0 == 0 and cc == 0:
                                norm(s, 2 * s.which)
                            if mods:
                                if cc < 7:
                                    mod_piece(s.sec, 1, i, cc)
                                if cc == 6:
                                    mod_piece(s.sec, 1, i, 7)
                                if cc == 7:
                                    mod_reduce(s.sec, 1, i)
                            if small:
                                merge(s, cc, 2 * t0 + cc, per, i)
                            if cc % 2 == 1:
                                dve.wait_ge(first_done, at(i, tiles, s.first + j + 1))
                                if o - 1 > 0:
                                    dve.wait_ge(oplo_done, at(i, tiles, o - 1))
                                if small:
                                    dve.wait_ge(merged_done, at(i, per, s.merged + 2 * t0 + cc + 1))
                                    src = HB[:, cc % BANK, :]
                                else:
                                    dve.wait_ge(unit_done, at(i, per, u0 + cc + 1))
                                    src = B[cc % BANK][:, 0:T]
                                V_.tensor_tensor(TMP[:, 2 + o % 2, 0:T], src, TMP[:, o % 2, 0:T], ALU.mult
                                                 ).then_inc(prod_done, 1)
                        if mods:
                            mod_store(s.sec, 1, i)
                    run(dve, s, body)
                elif s.kind == "down" or s.kind == "out":
                    pt = PER_TILE[s.kind]
                    first = [True]

                    set_gate(s, 5 if s.kind == "out" else 6 * s.which + 2, 1.0 if s.kind == "out" else 0.5)
                    clear_squares()

                    def body(i, t0, tiles, mods, u0, per):
                        for cc in range(per):
                            split_lo(u0 + cc + 1, per, i, next_words(s, cc, per))
                            if mods and cc < 8:
                                mod_piece(s.sec, 1, i, cc)
                            if mods and cc == 9:
                                mod_reduce(s.sec, 1, i)
                            if cc % pt == pt - 1:
                                n = t0 + cc // pt
                                residual(s, u0 + cc, per, n, tiles, i)
                                add_square(s.sq, n, tiles, i, T)
                        if mods:
                            mod_store(s.sec, 1, i)
                    run(dve, s, body)
                elif s.kind == "k" or s.kind == "q":
                    for cc in range(4):
                        split_lo(s.u + cc + 1, 0, 0)
                        if s.kind == "k" and cc == 0:
                            norm(s, 1)
                        if small:
                            merge(s, cc, cc, 0, 0, QTT[:, cc, 0:NX])
                elif s.kind == "v":
                    def heads2(ap):
                        return ap.rearrange("p (a n) -> p a n", a=1).broadcast_to([P, 2, NX])
                    cos, sin = heads2(CM[:, CM_COS:CM_COS + NX]), heads2(CM[:, CM_SIN:CM_SIN + NX])
                    dve.wait_ge(mixc_landed, 16 * (s.layer + 1))
                    for cc in range(8):
                        split_lo(s.u + cc + 1, 0, 0)
                        if cc % 2 == 1:
                            g = cc // 2
                            src = (KTT if g < 2 else QTT)[:, 2 * (g % 2):2 * (g % 2) + 2, 0:NX]
                            a = TMP[:, 0, :].rearrange("p (a n) -> p a n", a=2)
                            b = TMP[:, 1, :].rearrange("p (a n) -> p a n", a=2)
                            n = 4 * s.layer + g
                            if n > 0:
                                dve.wait_ge(rope_done, n)
                            dve.wait_ge(rot_done, n + 1)
                            dve.wait_ge(evac_done, s.evac)
                            V_.tensor_tensor(a, src, cos, ALU.mult).then_inc(rope_part, 1)
                            V_.tensor_tensor(b, B[4 + g][:].rearrange("p (a n) -> p a n", a=2), sin, ALU.mult
                                             ).then_inc(rope_part, 1)
                            dve.wait_ge(rope_part, 2 * n + 2)
                            V_.tensor_tensor(src, a, b, ALU.add).then_inc(rope_done, 1)
                        else:
                            h = cc // 2
                            e, dp = 4 * (HEADS * s.layer + h), 2 * (HEADS * s.layer + h)
                            for n, (g, op) in enumerate(((0, ALU.is_ge), (1, ALU.is_le))):
                                dve.wait_ge(exp_done, e + n + 1)
                                V_.scalar_tensor_tensor(G4[:, g, :], CM[:, CM_REL:CM_REL + 512], 0.0, G4[:, g, :],
                                                        op, ALU.mult).then_inc(dec_part, 1)
                            dve.wait_ge(dec_part, dp + 2)
                            V_.tensor_tensor(DEC[:, h, 0:2, :].rearrange("p a n -> p (a n)"), G4[:, 0, :], G4[:, 1, :],
                                             ALU.add).then_inc(dec_done, 1)
                            dve.wait_ge(exp_done, e + 4)
                            V_.tensor_tensor(DEC[:, h, 2:4, :].rearrange("p a n -> p (a n)"), G4[:, 2, :], G4[:, 3, :],
                                             ALU.add).then_inc(dec_done, 1)
                elif s.kind == "ret":
                    nP, nO = (2, 1) if small else (3, 2)
                    dve.wait_ge(dec_done, 2 * HEADS * (s.layer + 1))

                    def probs(h):
                        if h >= 2:
                            dve.wait_ge(ov_done, s.ov + nO * (h - 1))
                        for t in range(nP):
                            dve.wait_ge(score_done, s.score + nP * h + t + 1)
                            bank = B[2 * (h % 2) + t] if t < 2 else B[4]
                            dst = PX[:, h % 2, 2 * t:2 * t + 2, :] if t < 2 else PC[:, h % 2, :, :]
                            d = DEC[:, h, 2 * t:2 * t + 2, :] if t < 2 else DEC[:, h, 0:2, :]
                            V_.tensor_tensor(dst, bank[:].rearrange("p (a n) -> p a n", a=2), d, ALU.mult
                                             ).then_inc(mix_done, 1)

                    def head_norm(h):
                        reciprocal(s.ss + h, T)
                        for dv in range(2):
                            V_.tensor_tensor(O[:, 2 * h + dv, 0:T], O[:, 2 * h + dv, 0:T], RB[:, 0:T], ALU.mult
                                             ).then_inc(on_done, 1)

                    def head_sum(h):
                        dve.wait_ge(osq_done, HEADS * s.layer + h + 1)
                        t = TMP[:, 2 * (h % 2), 0:T]
                        V_.tensor_tensor(t, t, TMP[:, 2 * (h % 2) + 1, 0:T], ALU.add).then_inc(osum_done, 1)
                    probs(0)
                    probs(1)
                    probs(2)
                    head_sum(0)
                    probs(3)
                    head_sum(1)
                    head_norm(0)
                    head_sum(2)
                    head_norm(1)
                    head_sum(3)
                    head_norm(2)
                    head_norm(3)
                elif s.kind == "g":
                    def body(i, t0, tiles, mods, u0, per):
                        for cc in range(per):
                            o = s.o + cc
                            split_lo(u0 + cc + 1, per, i)
                            if small:
                                merge(s, cc, cc, per, i)
                            dve.wait_ge(first_done, at(i, per, s.first + cc + 1))
                            dve.wait_ge(oplo_done, at(i, per, o - 1))
                            dve.wait_ge(on_done, s.on)
                            V_.tensor_tensor(TMP[:, 2 + o % 2, 0:T], TMP[:, o % 2, 0:T],
                                             O[:, bass.ds(i * per + cc, 1), 0:T], ALU.mult).then_inc(prod_done, 1)
                    run(dve, s, body)
                elif s.kind == "conv":
                    segs = T // NX
                    dve.wait_ge(small_set, 3)

                    def body(i, t0, tiles, mods, u0, per):
                        for cc in range(per):
                            n, role = cc // 3, cc % 3
                            o = s.o + n
                            mx = s.mix + 4 * n
                            split_lo(u0 + cc + 1, per, i)
                            if mods and cc < 8:
                                mod_piece(s.sec, 1, i, cc)
                            if mods and cc == 9:
                                mod_reduce(s.sec, 1, i)
                            if small:
                                merge(s, cc, cc, per, i)
                            if role == 1:
                                if small:
                                    dve.wait_ge(merged_done, at(i, per, s.merged + cc + 1))
                                    a, b = HB[:, (cc - 1) % BANK, :], HB[:, cc % BANK, :]
                                else:
                                    dve.wait_ge(first_done, at(i, tiles, s.first + n + 1))
                                    dve.wait_ge(unit_done, at(i, per, u0 + cc + 1))
                                    a, b = TMP[:, n % 2, 0:T], B[cc % BANK][:, 0:T]
                                a, b = (v.rearrange("p (s n) -> p s n", s=segs) for v in (a, b))
                                dve.wait_ge(mix_done, at(i, 4 * tiles, mx))
                                dve.wait_ge(prod_done, at(i, tiles, o))
                                V_.tensor_tensor(U[:, 0:segs, 1:NX + 1], b, a, ALU.mult).then_inc(mix_done, 1)
                                acc = CV[:, 0:T].rearrange("p (s n) -> p s n", s=segs)
                                for tap in range(3):
                                    dve.wait_ge(mix_done, at(i, 4 * tiles, mx + 1 + tap))
                                    src = U[:, 0:segs, tap:tap + NX]
                                    wcol = VT_CONV + (3 * s.layer + tap) * KT + n
                                    w = VT[:, bass.ds(i * tiles + wcol, 1)]
                                    if tap == 0:
                                        V_.tensor_scalar(acc, src, w, None, ALU.mult).then_inc(mix_done, 1)
                                    else:
                                        V_.scalar_tensor_tensor(acc, src, w, acc, ALU.mult, ALU.add
                                                                ).then_inc(mix_done, 1)
                            if role == 2:
                                dve.wait_ge(mix_done, at(i, 4 * tiles, mx + 4))
                                dve.wait_ge(oplo_done, at(i, tiles, o - 1))
                                if small:
                                    dve.wait_ge(merged_done, at(i, per, s.merged + cc + 1))
                                    b = HB[:, cc % BANK, :]
                                else:
                                    dve.wait_ge(unit_done, at(i, per, u0 + cc + 1))
                                    b = B[cc % BANK][:, 0:T]
                                V_.tensor_tensor(TMP[:, 2 + o % 2, 0:T], b, CV[:, 0:T], ALU.mult
                                                 ).then_inc(prod_done, 1)
                        if mods:
                            mod_store(s.sec, 1, i)
                    run(dve, s, body)
                elif s.kind == "gates":
                    def body(i, t0, tiles, mods, u0, per):
                        for cc in range(per):
                            n, role = cc // 4, cc % 4
                            o = s.o + n
                            split_lo(u0 + cc + 1, per, i)
                            if small:
                                merge(s, cc, cc, per, i)
                            if role < 2:
                                continue
                            if small:
                                dve.wait_ge(merged_done, at(i, per, s.merged + cc + 1))
                                b = HB[:, cc % BANK, :]
                            else:
                                dve.wait_ge(unit_done, at(i, per, u0 + cc + 1))
                                b = B[cc % BANK][:, 0:T]
                            dve.wait_ge(first_done, at(i, 2 * tiles, s.first + 2 * n + role - 1))
                            if role == 2:
                                dve.wait_ge(oplo_done, at(i, tiles, o - 1))
                                V_.tensor_tensor(TMP[:, 2 + o % 2, 0:T], b, TMP[:, o % 2, 0:T], ALU.mult
                                                 ).then_inc(mix_done, 1)
                            else:
                                V_.tensor_tensor(CV[:, 0:T], b, CV[:, 0:T], ALU.mult).then_inc(mix_done, 1)
                                dve.wait_ge(mix_done, at(i, 2 * tiles, s.mix + 2 * n + 2))
                                V_.tensor_tensor(TMP[:, 2 + o % 2, 0:T], TMP[:, 2 + o % 2, 0:T], CV[:, 0:T], ALU.add
                                                 ).then_inc(prod_done, 1)
                    run(dve, s, body)
                else:
                    reciprocal(s.ss, T)
                    for k in range(KT):
                        if k >= 4:
                            dve.wait_ge(out_turned, 2 * (k - 3))
                        V_.scalar_tensor_tensor(TMP[:, k % 4, 0:T], H[:, k, 0:T], VT[:, VT_FINAL + k:VT_FINAL + k + 1],
                                                RB[:, 0:T], ALU.mult, ALU.mult).then_inc(y_done, 1)

        @block.gpsimd
        def _(pool):
            def lo(dst, full, hi, s, count, rate, i, done):
                pool.wait_ge(s, at(i, rate, count))
                nc.gpsimd.tensor_tensor(dst, full, hi.bitcast(F32), ALU.subtract).then_inc(done, 1)

            def y_lo(s):
                for k in range(KT):
                    lo(Y[:, k, 1, 0:s.T], TMP[:, k % 4, 0:s.T], Y[:, k, 0, 0:s.T], yhi_done, s.y + k + 1, 0, 0, ylo_done)

            for s in stages:
                T = s.T
                if s.kind == "k":
                    pool.wait_ge(unit_done, s.u)
                    pool.dma_start(CM[:], mix_in).then_inc(mixc_landed, 16)
                if s.kind in ("up", "k"):
                    y_lo(s)
                if s.kind in ("up", "g", "conv", "gates"):
                    X = {"up": Z, "g": R, "conv": C, "gates": M}[s.kind]

                    def body(i, t0, tiles, mods, u0, per):
                        for n in range(tiles):
                            o = s.o + t0 + n
                            at = bass.ds(i * tiles + t0 + n, 1)
                            lo(X[:, at, 1, 0:T], TMP[:, 2 + o % 2, 0:T], X[:, at, 0, 0:T],
                               ophi_done, o + 1, tiles, i, oplo_done)
                    run(pool, s, body)


_INS = ["x", "c", "ctx", "c_ctx", "norm_w", "w_mod", "b_mod", "ffn1_w_up", "ffn1_w_down", "w_in",
        "ret_log_decay", "conv_w", "w_ret_out", "w_conv_out", "w_out", "ffn2_w_up", "ffn2_w_down",
        "final_norm_w"]


def kernel(**inputs):
    import concourse.bacc as bacc
    from concourse.bass_utils import run_bass_kernel_spmd

    nc = bacc.Bacc("TRN2", target_bir_lowering=False, num_devices=1)
    arrays, args = {}, []
    tables = dict(zip(("keep", "mix"), constants()))
    for name in _INS + ["keep", "mix"]:
        a = np.ascontiguousarray(inputs[name] if name in inputs else tables[name])
        arrays[f"in_{name}_dram"] = a
        args.append(nc.dram_tensor(f"in_{name}_dram", a.shape, mybir.dt.from_np(a.dtype), kind="ExternalInput").ap())
    args.append(nc.dram_tensor("out_0_dram", (1, NX, D), F32, kind="ExternalOutput").ap())
    build(nc, *args)
    r = run_bass_kernel_spmd(nc, [arrays], core_ids=[0])
    return r.results[0]["out_0_dram"]
```

```python
import math
from contextlib import ExitStack

import numpy as np
import concourse.bass as bass
from concourse import mybir

F32 = mybir.dt.float32
F32R = mybir.dt.float32r
ACT = mybir.ActivationFunctionType
ALU = mybir.AluOpType
AXX = mybir.AxisListType.X

P = 128
D = 1024
KT = D // P
NX = 256
NC = 256
DEPTH = 2
HEADS, DK, DV = 4, 128, 256
FF = 2816
JF = FF // P
EPS = 1e-6
GRID_W = 64
ROPE_BASE = 10000.0
UW = 1024
RAW_SLOTS, HL_SLOTS = 4, 4
LEAD = 3
MOD0 = 4
SECTIONS = 9
COL_K, COL_V, COL_Q, COL_G, COL_CB, COL_CC, COL_CX, COL_GR, COL_GC = (
    0, 512, 1536, 2048, 3072, 4096, 5120, 6144, 7168)
VT_BMOD = (0, 128)
VT_NORM, VT_C, VT_CONV, VT_CCTX, VT_FINAL = 72, 120, 200, 248, 256
CK_ID, CK_QS, CK_COMB, CK_W = 0, 128, 256, 258
CM_COS, CM_SIN, CM_SWAP, CM_REL, CM_RELP, CM_RELN, CM_CF, CM_CB = (
    0, 256, 512, 640, 1152, 1664, 2176, 2688)
CM_W = 3200


def constants():
    p = np.arange(P)
    keep = np.zeros((P, CK_W), np.float32)
    keep[p, CK_ID + p] = 1.0
    keep[:, CK_QS:CK_QS + P] = (p[:, None] % 32 == p[None, :] % 32)
    keep[0:2, CK_COMB] = 1.0
    keep[2:4, CK_COMB + 1] = 1.0
    mix = np.zeros((P, CM_W), np.float32)
    tok = np.arange(NX)
    n_freq = DK // 4
    inv = (np.float32(ROPE_BASE) ** (-np.arange(n_freq, dtype=np.float32) / np.float32(n_freq))).astype(np.float32)
    pos = np.stack([tok // GRID_W, tok % GRID_W]).astype(np.float32)
    ang = pos[p // 64][:, :] * inv[p % 32][:, None]
    sign = np.where((p // 32) % 2 == 0, -1.0, 1.0).astype(np.float32)[:, None]
    mix[:, CM_COS:CM_COS + NX] = np.cos(ang)
    mix[:, CM_SIN:CM_SIN + NX] = np.sin(ang) * sign
    mix[p, CM_SWAP + (p ^ 32)] = 1.0
    key = (np.arange(2)[None, :, None] * P + p[:, None, None]).astype(np.float32)
    q = tok[None, None, :].astype(np.float32)
    rel = (q - key).reshape(P, 512)
    mix[:, CM_REL:CM_REL + 512] = rel
    mix[:, CM_RELP:CM_RELP + 512] = np.maximum(rel, 0)
    mix[:, CM_RELN:CM_RELN + 512] = np.maximum(-rel, 0)
    mix[:, CM_CF:CM_CF + 512] = (q + NC - key).reshape(P, 512)
    mix[:, CM_CB:CM_CB + 512] = (NX - q + key).reshape(P, 512)
    return keep, mix


class Stage:

    def __init__(self, kind, layer, T, n, at, entry, which=0, mods=None, last=False):
        self.kind, self.layer, self.T, self.n, self.entry = kind, layer, T, n, entry
        self.which, self.mods, self.last = which, mods, last
        self.u, self.o, self.h = at["u"], at["o"], at["h"]
        self.first, self.half, self.merged = at["first"], at["half"], at["merged"]
        self.mix, self.sq, self.evac = at["mix"], at["sq"], at["evac"]
        self.sec, self.ss, self.y = at["sec"], at["ss"], at["y"]
        self.score, self.ov, self.on, self.rot = at["score"], at["ov"], at["on"], at["rot"]
        self.hpart = at["hpart"]
        self.mods_end = mods == 1 and kind == "down"


COUNTERS = ("u", "o", "first", "half", "merged", "mix", "h", "sq", "evac", "sec", "ss", "y",
            "score", "ov", "on", "rot", "hpart")


def plan():
    at = {name: 0 for name in COUNTERS}
    stages, free = [], []

    def add(kind, layer, T, n, adds, frees, **kw):
        nonlocal free
        s = Stage(kind, layer, T, n, at, list(free), **kw)
        for k, v in adds.items():
            at[k] += v
        free = [(f, at[f]) for f in frees]
        stages.append(s)

    add("ada", 0, NX + NC, 2, dict(u=2 * KT, h=KT, sq=KT + 1, sec=2), [])
    for layer in range(DEPTH):
        last = layer == DEPTH - 1
        T2 = NX if last else NX + NC

        def ffn(which, T, mods):
            mods_up = 5 if mods is not None else 0
            small = T == NX
            add("up", layer, T, JF, dict(u=2 * JF, o=JF, first=JF, ss=1, y=KT, sec=mods_up,
                                         **({"half": 2 * JF, "merged": 2 * JF} if small else {})),
                ["merged"] if small else ["first", "o"], which=which, mods=mods)
            add("down", layer, T, KT, dict(u=3 * KT, h=KT, hpart=KT, sq=KT + 1, sec=2 if mods is not None else 0),
                ["h"], which=which, mods=mods, last=last and which == 1)

        ffn(0, NX + NC, 0 if not last else None)
        small = T2 == NX
        add("k", layer, NX + NC, 4, dict(u=4, evac=4, ss=1, y=KT), ["evac"])
        if small:
            add("q", layer, T2, 4, dict(u=4, half=4, merged=4), ["merged"])
        else:
            add("q", layer, T2, 4, dict(u=4, evac=4), ["evac"])
        add("v", layer, NX + NC, 8, dict(u=8, evac=8, rot=4), ["evac"])
        nP, nO = (2, 1) if small else (3, 2)
        add("ret", layer, T2, HEADS,
            dict(mix=nP * HEADS, score=nP * HEADS, ov=nO * HEADS, evac=nO * HEADS, ss=HEADS, on=2 * HEADS),
            ["mix", "evac"])
        hm = lambda k: {"half": k, "merged": k} if small else {}
        add("g", layer, T2, KT, dict(u=8, o=8, first=8, **hm(8)), ["merged"] if small else ["first"])
        add("conv", layer, T2, KT, dict(u=24, o=8, mix=32, sec=0 if last else 2,
                                        **({} if small else {"first": 8}), **hm(24)),
            ["merged"] if small else ["first", "mix", "o"], mods=None if last else 1)
        add("gates", layer, T2, KT, dict(u=32, o=8, first=16, mix=16, **hm(32)),
            ["merged"] if small else ["first", "mix"])
        add("out", layer, T2, KT, dict(u=8, h=KT, hpart=KT, sq=KT + 1), ["h"])
        ffn(1, T2, 1 if not last else None)
    add("final", DEPTH - 1, NX, 0, dict(ss=1), [])
    return stages, at


def build(nc, x, c, ctx_in, c_ctx, norm_w, w_mod, b_mod, up1, down1, w_in, log_decay, conv_w,
          w_ret, w_conv, w_out, up2, down2, final_w, keep_in, mix_in, out):
    stages, totals = plan()
    es = ExitStack()
    cursor = [1152]

    def place(name, shape, dt=F32, at=None):
        size = 4 * int(np.prod(shape[1:]))
        if at is None:
            at = cursor[0]
            cursor[0] += (size + 31) // 32 * 32
        return nc.alloc_sbuf_tensor_at(name, shape, dt, offset=at)

    H = place("H", [P, KT, 512])
    Y = place("Y", [P, KT, 2, 512], F32R)
    zone = cursor[0]
    cursor[0] += 98304
    Z = place("Z", [P, JF, 2, 512], F32R, zone)
    R = place("R", [P, KT, 2, 512], F32R, zone)
    CM = place("CM", [P, CM_W], F32, zone)
    G4 = place("G4", [P, 4, 512], F32, zone + 4 * CM_W)
    PX = place("PX", [P, 2, 4, 256], F32, zone + 4 * CM_W)
    PC = place("PC", [P, 2, 2, 256], F32, zone + 4 * CM_W + 8192)
    C = place("C", [P, KT, 2, 512], F32R, zone + 32768)
    DEC = place("DEC", [P, HEADS, 4, 256], F32, zone + 32768)
    O = place("O", [P, KT, 512], F32, zone + 32768 + 16384)
    KTT = place("KTT", [P, HEADS, 512], F32, zone + 65536)
    QTT = place("QTT", [P, HEADS, 512], F32, zone + 65536 + 8192)
    V = place("V", [P, 4, HEADS * DV], F32, zone + 65536 + 16384)
    M = place("M", [P, KT, 2, 512], F32R, zone + 65536)
    MODRAW = [place(f"MODRAW{s}", [P, UW], F32, zone + 90112 + 4096 * s) for s in range(2)]
    XROWS = place("XROWS", [P, 4, D], F32, zone)
    VROWS = place("VROWS", [P, 3, P], F32, zone + 16384)
    SCP = place("SCP", [P, KT, P], F32R, zone + 20480)
    ADAROWS = place("ADAROWS", [P, 2 * D], F32, zone + 24576)
    OROWS = place("OROWS", [P, 2, D], F32, zone)
    RAW = [place(f"RAW{s}", [P, UW]) for s in range(RAW_SLOTS)]
    HI = [place(f"HI{s}", [P, UW], F32R) for s in range(HL_SLOTS)]
    LO = [place(f"LO{s}", [P, UW], F32R) for s in range(HL_SLOTS)]
    TMP = place("TMP", [P, 4, 512])
    SQACC = place("SQACC", [P, 512])
    RB = place("RB", [P, 512])
    CV = place("CV", [P, 512])
    U = place("U", [P, 2, 258])
    MODACC = place("MODACC", [P, 2, UW])
    HB = place("HB", [P, 4, 256], F32, cursor[0] - 8192)
    MT = place("MT", [P, 512])
    MR = place("MR", [P, 64])
    CK = place("CK", [P, CK_W])
    ONES = place("ONES", [P, P])
    VT = place("VT", [P, 264])
    MODS = place("MODS", [P, 1 + DEPTH * SECTIONS, 2, KT])
    AMUL = place("AMUL", [P, 2, KT])
    GATE = place("GATE", [P, 2, KT])
    SC = place("SC", [P, 2, KT])
    LG = place("LG", [P, DEPTH * 2 * HEADS])
    EPST = place("EPST", [P, 1])
    assert cursor[0] <= nc.sbuf_usable_end, cursor[0]

    with es:
        B = [es.enter_context(nc.psum_tensor(f"bank{i}", [P, 512], F32)) for i in range(8)]
        names = {}

        def sem(name):
            names[name] = es.enter_context(nc.semaphore(name))
            return names[name]

        raw_landed = [sem(f"raw_landed{s}") for s in range(RAW_SLOTS)]
        mod_landed = [sem(f"mod_landed{s}") for s in range(2)]
        vec_landed, const_landed, x_landed, mixc_landed = (
            sem("vec_landed"), sem("const_landed"), sem("x_landed"), sem("mixc_landed"))
        hi_done, lo_done, unit_done = sem("hi_done"), sem("lo_done"), sem("unit_done")
        first_done, prod_done, ophi_done, oplo_done = (
            sem("first_done"), sem("prod_done"), sem("ophi_done"), sem("oplo_done"))
        half_done, merged_done, mix_done = sem("half_done"), sem("merged_done"), sem("mix_done")
        h_done, sq_done, sqsum_done = sem("h_done"), sem("sq_done"), sem("sqsum_done")
        ss_done, rt_done, rb_done = sem("ss_done"), sem("rt_done"), sem("rb_done")
        y_scaled, y_done, yhi_done, ylo_done = (
            sem("y_scaled"), sem("y_done"), sem("yhi_done"), sem("ylo_done"))
        evac_done, rot_done, rope_part, rope_done = (
            sem("evac_done"), sem("rot_done"), sem("rope_part"), sem("rope_done"))
        exp_done, dec_part, dec_done = sem("exp_done"), sem("dec_part"), sem("dec_done")
        score_done, ov_done, osq_done, osum_done, on_done = (
            sem("score_done"), sem("ov_done"), sem("osq_done"), sem("osum_done"), sem("on_done"))
        mod_step, mod_fin, mod_sum, mods_ready, amul_done = (
            sem("mod_step"), sem("mod_fin"), sem("mod_sum"), sem("mods_ready"), sem("amul_done"))
        small_set, vec_turned, vt_done, sc_done, x_turned = (
            sem("small_set"), sem("vec_turned"), sem("vt_done"), sem("sc_done"), sem("x_turned"))
        scp_hi, scp_lo, ada_rows, ada_turned = sem("scp_hi"), sem("scp_lo"), sem("ada_rows"), sem("ada_turned")
        out_turned, out_copied, out_stored = sem("out_turned"), sem("out_copied"), sem("out_stored")
        block = es.enter_context(nc.Block())
        FREES = {"first": first_done, "o": prod_done, "merged": merged_done, "h": h_done,
                 "evac": evac_done, "mix": mix_done}

        start = [0]

        def at(i, rate, base):
            if isinstance(i, int):
                return base + rate * i
            return i * rate + (base - rate * start[0])

        def raw_wait(eng, u, per, i):
            eng.wait_ge(raw_landed[u % RAW_SLOTS], at(i, 16 * per // RAW_SLOTS, 16 * (u // RAW_SLOTS + 1)))

        def loops(s):
            if s.kind == "up":
                parts = [(None, 0, 2, False), (5, 2, 4, s.mods is not None)]
            elif s.kind == "down":
                if s.last:
                    parts = [(None, 0, 4, False), (None, 4, 4, False)]
                else:
                    parts = [(2, 0, 4, s.mods is not None)]
            elif s.kind == "conv":
                parts = [(2, 0, 4, s.mods is not None)]
            elif s.kind == "g" or s.kind == "out":
                parts = [(2, 0, 4, False)]
            elif s.kind == "gates":
                parts = [(4, 0, 2, False)]
            elif s.kind in ("k", "q"):
                parts = [(None, 0, 4, False)]
            else:
                raise ValueError(s.kind)
            return parts

        PER_TILE = {"up": 2, "down": 3, "conv": 3, "g": 1, "out": 1, "gates": 4, "k": 1, "q": 1}
        BANK = 4

        def run(eng, s, body):
            for count, t0, tiles, mods in loops(s):
                per = tiles * PER_TILE[s.kind]
                u0 = s.u + t0 * PER_TILE[s.kind]
                if count is None:
                    body(0, t0, tiles, mods, u0, per)
                else:
                    first = 1 if eng is nc.sync and s.kind != "up" else 0
                    start[0] = first
                    with eng.Fori(first, first + count) as i:
                        body(i, t0, tiles, mods, u0, per)
                    start[0] = 0

        def unit_words(s, c):
            return (JF - 2 * KT) * P if s.kind == "down" and c % 3 == 2 else UW

        last_u = totals["u"]
        UP, DOWN = (up1, up2), (down1, down2)

        @block.sync
        def _(sp):
            def load(u, per, i, src, words=UW):
                if u - RAW_SLOTS + 1 > 0:
                    sp.wait_ge(lo_done, at(i, per, u - RAW_SLOTS + 1))
                dst = RAW[u % RAW_SLOTS][:, 0:words].rearrange("p (k n) -> p k n", k=src.shape[1])
                sp.dma_start(dst, src).then_inc(raw_landed[u % RAW_SLOTS], 16)

            def block_of(w, k0, nk, col):
                v = w.rearrange("(k p) n -> p k n", p=P)
                return v[:, k0:k0 + nk, bass.ds(col, P)]

            row = 0
            for g, parts in enumerate((
                    ((b_mod[0], 0), (norm_w.rearrange("l i d -> (l i d)"), 72), (c[0], 120)),
                    ((b_mod[1], 0), (conv_w.rearrange("l i d -> (l i d)"), 72), (c_ctx, 120)),
                    ((final_w, 0),))):
                for src, r in parts:
                    rows = src.rearrange("(r p) -> r p", p=P)
                    sp.dma_start(VROWS[r:r + rows.shape[0], g, :], rows).then_inc(vec_landed, 16)
            sp.dma_start(CK[:], keep_in).then_inc(const_landed, 16)
            lg = log_decay.rearrange("l d h -> (l d h)")
            sp.dma_start(LG[:], lg.partition_broadcast(P)).then_inc(const_landed, 16)

            for s in stages:
                if s.kind == "ada":
                    w = w_mod[0].rearrange("(k p) n -> p k n", p=P)
                    for cc in range(2 * KT):
                        load(s.u + cc, 0, 0, w[:, cc % KT:cc % KT + 1, (cc // KT) * D:(cc // KT + 1) * D])
                        if cc == 1:
                            for t, src in enumerate((x[0], ctx_in[0])):
                                sp.dma_start(XROWS[:, 2 * t:2 * t + 2, :], src.rearrange("(t p) d -> p t d", p=P)
                                             ).then_inc(x_landed, 16)
                elif s.kind == "up":
                    w = UP[s.which][s.layer]

                    def body(i, t0, tiles, mods, u0, per):
                        for cc in range(per):
                            col = at(i, tiles * P, (t0 + cc // 2) * P + (cc % 2) * FF)
                            load(u0 + cc, per, i, block_of(w, 0, KT, col))
                    run(sp, s, body)
                elif s.kind == "down":
                    w = DOWN[s.which][s.layer]

                    def body(i, t0, tiles, mods, u0, per):
                        for cc in range(per):
                            k0 = KT * (cc % 3)
                            load(u0 + cc, per, i, block_of(w, k0, min(KT, JF - k0), at(i, tiles * P, (t0 + cc // 3) * P)),
                                 unit_words(s, cc))
                    run(sp, s, body)
                elif s.kind in ("k", "q", "g", "out", "conv", "gates"):
                    wl = w_in[s.layer]
                    parts = {"k": [(wl, COL_K)], "q": [(wl, COL_Q)], "g": [(wl, COL_G)],
                             "conv": [(wl, COL_CC), (wl, COL_CX), (wl, COL_CB)],
                             "gates": [(wl, COL_GR), (wl, COL_GC), (w_ret[s.layer], 0), (w_conv[s.layer], 0)],
                             "out": [(w_out[s.layer], 0)]}[s.kind]

                    def body(i, t0, tiles, mods, u0, per):
                        for cc in range(per):
                            w, base = parts[cc % len(parts)]
                            load(u0 + cc, per, i, block_of(w, 0, KT, at(i, tiles * P, base + (cc // len(parts)) * P)))
                    run(sp, s, body)
                elif s.kind == "v":
                    v = w_in[s.layer].rearrange("(k p) n -> p k n", p=P)
                    for cc in range(8):
                        half, kp = cc // 4, cc % 4
                        load(s.u + cc, 0, 0, v[:, 2 * kp:2 * kp + 2, COL_V + 512 * half:COL_V + 512 * half + 512])
                elif s.kind == "final":
                    sp.wait_ge(out_copied, 4)
                    sp.dma_start(out[0].rearrange("(t p) d -> p t d", p=P), OROWS[:]).then_inc(out_stored, 16)
                    sp.wait_ge(out_stored, 16)

        @block.tensor
        def _(pe):
            mm = nc.tensor.matmul

            def block_mm(bank, slot, kk, X, k, T, first, last):
                hi, lo = HI[slot][:, kk * P:(kk + 1) * P], LO[slot][:, kk * P:(kk + 1) * P]
                if T == 512:
                    mm(bank[:], hi, X[:, k, 0, :], start=first, stop=False)
                    mm(bank[:], hi, X[:, k, 1, :], start=False, stop=False)
                    return mm(bank[:], lo, X[:, k, 0, :], start=False, stop=last)
                mm(bank[:], hi, X[:, k, :, 0:NX], start=first, stop=False)
                return mm(bank[:, 0:NX], lo, X[:, k, 0, 0:NX], start=False, stop=last)

            def unit(u, per, i, bank, X, k0, nk, T, first=True, last=True):
                slot = u % HL_SLOTS
                pe.wait_ge(lo_done, at(i, per, u + 1))
                for kk in range(nk):
                    ins = block_mm(bank, slot, kk, X, k0 + kk, T, first and kk == 0, last and kk == nk - 1)
                ins.then_inc(unit_done, 1)

            def first_two(s):
                pe.wait_ge(lo_done, s.u + 2)
                for k in range(KT):
                    if s.T == 512:
                        pe.wait_ge(yhi_done, s.y + k + 1)
                        for uu in range(2):
                            for w in (HI, LO):
                                mm(B[uu][:], w[(s.u + uu) % HL_SLOTS][:, k * P:(k + 1) * P], Y[:, k, 0, :],
                                   start=(k == 0 and w is HI), stop=False)
                        pe.wait_ge(ylo_done, s.y + k + 1)
                        for uu in range(2):
                            ins = mm(B[uu][:], HI[(s.u + uu) % HL_SLOTS][:, k * P:(k + 1) * P], Y[:, k, 1, :],
                                     start=False, stop=(k == KT - 1))
                            if k == KT - 1:
                                ins.then_inc(unit_done, 1)
                        continue
                    pe.wait_ge(ylo_done, s.y + k + 1)
                    for uu in range(2):
                        ins = block_mm(B[uu], (s.u + uu) % HL_SLOTS, k, Y, k, s.T, k == 0, k == KT - 1)
                        if k == KT - 1:
                            ins.then_inc(unit_done, 1)

            def keep_clock(n):
                for _ in range(n):
                    mm(B[6][:, 0:P], ONES[:], ONES[:], start=True, stop=True)

            def sumsq(s):
                keep_clock(8)
                pe.wait_ge(sqsum_done, s.sq)
                mm(B[4][:, 0:s.T], ONES[:], SQACC[:, 0:s.T], start=True, stop=True).then_inc(ss_done, 1)
                if s.kind != "final":
                    keep_clock(22)

            def mod_total(sec, rate, i):
                pe.wait_ge(mod_fin, at(i, 8 * rate, 8 * (sec - 1)))
                mm(B[5][:, 0:64], CK[:, CK_QS:CK_QS + P], MR[:], start=True, stop=True).then_inc(mod_sum, 1)

            pe.wait_ge(vec_landed, 16 * 7)
            pe.wait_ge(const_landed, 32)
            pe.wait_ge(small_set, 2)
            ident = CK[:, CK_ID:CK_ID + P]
            for g in range(3):
                n = P if g < 2 else KT
                nc.tensor.transpose(B[4 + g][:, 0:n], VROWS[0:n, g, :], ident[0:n, 0:n]).then_inc(vec_turned, 1)
            for s in stages:
                for name, count in s.entry:
                    pe.wait_ge(FREES[name], count)
                small = s.T == NX
                if s.kind == "ada":
                    pe.wait_ge(scp_lo, 1)
                    for cc in range(2 * KT):
                        u, k = s.u + cc, cc % KT
                        pe.wait_ge(lo_done, u + 1)
                        for half in range(2):
                            bank = B[2 * (cc // KT) + half]
                            cols = slice(half * 512, (half + 1) * 512)
                            mm(bank[:], SCP[:, k, :], HI[u % HL_SLOTS][:, cols], start=(k == 0), stop=False)
                            ins = mm(bank[:], SCP[:, k, :], LO[u % HL_SLOTS][:, cols], start=False, stop=(k == KT - 1))
                        ins.then_inc(unit_done, 1)
                        if cc in (5, 9):
                            if cc == 5:
                                pe.wait_ge(x_landed, 32)
                                pe.wait_ge(vt_done, 3)
                            else:
                                pe.wait_ge(h_done, 4)
                            for q in range(4):
                                k4 = q + (0 if cc == 5 else 4)
                                for t in range(4):
                                    ins = nc.tensor.transpose(B[4 + q][:, t * P:(t + 1) * P],
                                                              XROWS[:, t, k4 * P:(k4 + 1) * P], ident)
                                ins.then_inc(x_turned, 1)
                    pe.wait_ge(h_done, KT)
                    pe.wait_ge(ada_rows, 4)
                    for m in range(2 * KT):
                        ins = mm(B[5][:, 2 * m:2 * m + 2], ADAROWS[0:4, m * P:(m + 1) * P],
                                 CK[0:4, CK_COMB:CK_COMB + 2], start=True, stop=True)
                    ins.then_inc(ada_turned, 1)
                elif s.kind == "up":
                    sumsq(s)
                    first_two(s)

                    def body(i, t0, tiles, mods, u0, per):
                        for cc in range(per):
                            if t0 == 0 and cc < 2:
                                continue
                            if mods and cc == 4:
                                mod_total(s.sec, 1, i)
                            j = t0 + cc // 2
                            if small:
                                pe.wait_ge(merged_done, at(i, per, s.merged + 2 * t0 + cc - BANK + 1))
                            elif cc % 2 == 0:
                                if s.first + j - 1 > 0:
                                    pe.wait_ge(first_done, at(i, tiles, s.first + j - 1))
                            else:
                                if s.o + j - 1 > 0:
                                    pe.wait_ge(prod_done, at(i, tiles, s.o + j - 1))
                            unit(u0 + cc, per, i, B[cc % BANK], Y, 0, KT, s.T)
                    run(pe, s, body)
                elif s.kind == "down":
                    def body(i, t0, tiles, mods, u0, per):
                        for cc in range(per):
                            n, part = t0 + cc // 3, cc % 3
                            if mods and cc == 4:
                                mod_total(s.sec, 1, i)
                            if part == 0:
                                pe.wait_ge(h_done, at(i, tiles, s.h + n - BANK + 1))
                            pe.wait_ge(oplo_done, s.o - JF + min(JF, KT * (part + 1)))
                            nk = min(KT, JF - KT * part)
                            unit(u0 + cc, per, i, B[n % BANK], Z, KT * part, nk, s.T, part == 0, part == 2)
                    run(pe, s, body)
                    if s.mods_end:
                        mod_total(DEPTH * SECTIONS, 0, 0)
                elif s.kind == "k":
                    sumsq(s)
                    first_two(s)
                    for cc in (2, 3):
                        unit(s.u + cc, 0, 0, B[cc], Y, 0, KT, s.T)
                elif s.kind == "q":
                    for cc in range(4):
                        unit(s.u + cc, 0, 0, B[cc], Y, 0, KT, s.T)
                elif s.kind == "v":
                    def rots(first, src):
                        for g in range(2):
                            mm(B[4 + first + g][:], CM[:, CM_SWAP:CM_SWAP + P], src[:, 2 * g:2 * g + 2, 0:NX],
                               start=True, stop=True).then_inc(rot_done, 1)
                    pe.wait_ge(mixc_landed, 16 * (s.layer + 1))
                    rots(0, KTT)
                    for cc in range(8):
                        half, kp = cc // 4, cc % 4
                        u = s.u + cc
                        pe.wait_ge(lo_done, u + 1)
                        for kk in range(2):
                            k = 2 * kp + kk
                            for tt in range(4):
                                if half == 1 and k == 0:
                                    pe.wait_ge(evac_done, s.evac + tt + 1)
                                for a, w in ((0, HI), (0, LO), (1, HI)):
                                    ins = mm(B[tt][:], Y[:, k, a, tt * P:(tt + 1) * P],
                                             w[u % HL_SLOTS][:, kk * 512:(kk + 1) * 512],
                                             start=(k == 0 and (a, w) == (0, HI)), stop=(k == KT - 1 and a == 1))
                        ins.then_inc(unit_done, 1)
                        if cc == 0:
                            rots(2, QTT)
                elif s.kind == "ret":
                    nP, nO = (2, 1) if small else (3, 2)
                    pe.wait_ge(rope_done, 4 * (s.layer + 1))

                    def scores(h):
                        if h >= 2:
                            pe.wait_ge(mix_done, s.mix + nP * (h - 1))
                        for half in range(2):
                            bank = B[2 * (h % 2) + half]
                            for q in range(2):
                                j = 2 * half + q
                                ins = mm(bank[:, q * NX:(q + 1) * NX], KTT[:, h, j * P:(j + 1) * P], QTT[:, h, 0:NX],
                                         start=True, stop=True)
                            ins.then_inc(score_done, 1)
                        if not small:
                            if h:
                                pe.wait_ge(mix_done, s.mix + nP * h)
                            for q in range(2):
                                ins = mm(B[4][:, q * NX:(q + 1) * NX], KTT[:, h, NX + q * P:NX + (q + 1) * P],
                                         QTT[:, h, NX:NX + NC], start=True, stop=True)
                            ins.then_inc(score_done, 1)

                    def outputs(h):
                        pe.wait_ge(mix_done, s.mix + nP * (h + 1))
                        if h:
                            pe.wait_ge(evac_done, s.evac + nO * h)
                        for dv in range(2):
                            for j in range(4):
                                ins = mm(B[5][:, dv * NX:(dv + 1) * NX],
                                         V[:, j, h * DV + dv * P:h * DV + (dv + 1) * P], PX[:, h % 2, j, :],
                                         start=(j == 0), stop=(j == 3))
                        ins.then_inc(ov_done, 1)
                        if not small:
                            for dv in range(2):
                                for j in range(2):
                                    ins = mm(B[6][:, dv * NX:(dv + 1) * NX],
                                             V[:, 2 + j, h * DV + dv * P:h * DV + (dv + 1) * P], PC[:, h % 2, j, :],
                                             start=(j == 0), stop=(j == 1))
                            ins.then_inc(ov_done, 1)

                    def head_sumsq(h):
                        pe.wait_ge(osum_done, HEADS * s.layer + h + 1)
                        pe.wait_ge(rt_done, s.ss + h)
                        mm(B[7][:, 0:s.T], ONES[:], TMP[:, 2 * (h % 2), 0:s.T], start=True, stop=True
                           ).then_inc(ss_done, 1)

                    scores(0)
                    scores(1)
                    outputs(0)
                    scores(2)
                    outputs(1)
                    head_sumsq(0)
                    scores(3)
                    outputs(2)
                    head_sumsq(1)
                    outputs(3)
                    head_sumsq(2)
                    head_sumsq(3)
                elif s.kind == "g":
                    def body(i, t0, tiles, mods, u0, per):
                        for cc in range(per):
                            if small:
                                pe.wait_ge(merged_done, at(i, per, s.merged + cc - BANK + 1))
                            else:
                                pe.wait_ge(first_done, at(i, per, s.first + cc - BANK + 1))
                            unit(u0 + cc, per, i, B[cc % BANK], Y, 0, KT, s.T)
                    run(pe, s, body)
                elif s.kind == "conv":
                    def body(i, t0, tiles, mods, u0, per):
                        for cc in range(per):
                            n, role = (cc - BANK) // 3, (cc - BANK) % 3
                            if mods and cc == 4:
                                mod_total(s.sec, 1, i)
                            if small:
                                pe.wait_ge(merged_done, at(i, per, s.merged + cc - BANK + 1))
                            elif role == 0:
                                pe.wait_ge(first_done, at(i, tiles, s.first + n + 1))
                            elif role == 1:
                                pe.wait_ge(mix_done, at(i, 4 * tiles, s.mix + 4 * n + 1))
                            else:
                                pe.wait_ge(prod_done, at(i, tiles, s.o + n + 1))
                            unit(u0 + cc, per, i, B[cc % BANK], Y, 0, KT, s.T)
                    run(pe, s, body)
                elif s.kind == "gates":
                    pe.wait_ge(oplo_done, s.o)
                    src = (Y, Y, R, C)

                    def body(i, t0, tiles, mods, u0, per):
                        for cc in range(per):
                            n, role = cc // 4 - 1, cc % 4
                            if small:
                                pe.wait_ge(merged_done, at(i, per, s.merged + cc - BANK + 1))
                            elif role < 2:
                                pe.wait_ge(first_done, at(i, 2 * tiles, s.first + 2 * n + role + 1))
                            else:
                                pe.wait_ge(mix_done, at(i, 2 * tiles, s.mix + 2 * n + role - 1))
                            unit(u0 + cc, per, i, B[cc % BANK], src[role], 0, KT, s.T)
                    run(pe, s, body)
                elif s.kind == "out":
                    pe.wait_ge(oplo_done, s.o)

                    def body(i, t0, tiles, mods, u0, per):
                        for cc in range(per):
                            pe.wait_ge(h_done, at(i, per, s.h + cc - BANK + 1))
                            unit(u0 + cc, per, i, B[cc % BANK], M, 0, KT, s.T)
                    run(pe, s, body)
                else:
                    sumsq(s)
                    for k in range(KT):
                        pe.wait_ge(y_done, s.y + k + 1)
                        for t in range(2):
                            nc.tensor.transpose(B[2 * t + k // 4][:, (k % 4) * P:(k % 4 + 1) * P],
                                                TMP[:, k % 4, t * P:(t + 1) * P],
                                                ident).then_inc(out_turned, 1)

        @block.scalar
        def _(act):
            A = nc.scalar.activation

            def split_hi(u, per, i, words=UW):
                if u >= last_u and isinstance(i, int):
                    return
                raw_wait(act, u, per, i)
                if u - HL_SLOTS + 1 > 0:
                    act.wait_ge(unit_done, at(i, per, u - HL_SLOTS + 1))
                A(HI[u % HL_SLOTS][:, 0:words], RAW[u % RAW_SLOTS][:, 0:words], ACT.Copy).then_inc(hi_done, 1)

            def next_words(s, cc, per):
                return unit_words(s, cc + LEAD) if cc + LEAD < per else UW

            def square(base_h, base_sq, n, rate, i, src_tile, T):
                act.wait_ge(h_done, at(i, rate, base_h + n + 1))
                if base_sq + n > 0:
                    act.wait_ge(sqsum_done, at(i, rate, base_sq + n))
                A(TMP[:, n % 2, 0:T], src_tile, ACT.Square).then_inc(sq_done, 1)

            def root(s_ss, n, T, ss_bank):
                act.wait_ge(ss_done, s_ss + 1)
                A(RB[:, 0:T], ss_bank[:, 0:T], ACT.Sqrt, bias=EPST[:, 0:1], scale=1.0 / n).then_inc(rt_done, 1)

            def y_hi(s):
                root(s.ss, D, s.T, B[4])
                for k in range(KT):
                    act.wait_ge(y_done, s.y + k + 1)
                    A(Y[:, k, 0, 0:s.T], TMP[:, k % 4, 0:s.T], ACT.Copy).then_inc(yhi_done, 1)

            def half_copy(s, u, per, i, c, rel, o_wait, o_rate):
                act.wait_ge(unit_done, at(i, per, u + 1))
                act.wait_ge(prod_done, at(i, o_rate, o_wait))
                A(HB[:, c % BANK, :], B[c % BANK][:, NX:2 * NX], ACT.Copy).then_inc(half_done, 1)

            def operand_hi(o, rate, i, dst, T):
                act.wait_ge(prod_done, at(i, rate, o + 1))
                A(dst, TMP[:, 2 + o % 2, 0:T], ACT.Copy).then_inc(ophi_done, 1)

            def mod_load(sec, rate, i, k):
                act.wait_ge(mod_step, at(i, 16 * rate, MOD0 + 2 * (8 * (sec - 2) + k - 1)))
                layer, within = sec // SECTIONS, sec % SECTIONS
                act.dma_start(MODRAW[k % 2][:], w_mod[layer][k * P:(k + 1) * P, bass.ds(at(i, UW * rate, within * UW), UW)]
                              ).then_inc(mod_landed[k % 2], 16)

            def mod_loads(s, cc, i):
                for k in ((0, 1) if cc == 0 else (cc + 1,) if cc + 1 < KT else ()):
                    mod_load(s.sec, 1, i, k)

            act.wait_ge(vt_done, 2)
            A(SC[:, 0, :], VT[:, VT_C:VT_C + KT], ACT.Silu)
            A(SC[:, 1, :], VT[:, VT_CCTX:VT_CCTX + KT], ACT.Silu).then_inc(sc_done, 1)
            act.wait_ge(sc_done, 1)
            act.wait_ge(small_set, 4)
            for cond in range(2):
                A(SCP[:, :, 2 * cond], SC[:, cond, :], ACT.Copy).then_inc(scp_hi, 1)
            for u in range(LEAD):
                split_hi(u, 0, 0)

            for s in stages:
                T, small = s.T, s.T == NX
                if s.kind == "ada":
                    for cc in range(2 * KT):
                        split_hi(s.u + cc + LEAD, 0, 0)
                        if cc in (6, 10):
                            for k in range(0 if cc == 6 else 4, 4 if cc == 6 else 8):
                                square(0, 0, k, 0, 0, H[:, k, :], 512)
                    act.wait_ge(unit_done, s.u + 2 * KT)
                    for b in (1, 3):
                        A(ADAROWS[0:4, b * 512:(b + 1) * 512], B[b][0:4, :], ACT.Copy).then_inc(ada_rows, 1)
                elif s.kind == "up":
                    def body(i, t0, tiles, mods, u0, per):
                        for cc in range(per):
                            j, jj = t0 + cc // 2, cc // 2
                            if small and t0 + cc:
                                half_copy(s, u0 + cc, per, i, cc, 0, s.o + j - 1, tiles)
                            split_hi(u0 + cc + LEAD, per, i)
                            if mods:
                                mod_loads(s, cc, i)
                            if t0 == 0 and cc == 0:
                                y_hi(s)
                                if small:
                                    half_copy(s, u0, per, i, 0, 0, s.o - 1, tiles)
                            if cc % 2 == 0:
                                if small:
                                    act.wait_ge(merged_done, at(i, per, s.merged + 2 * t0 + cc + 1))
                                    src = HB[:, cc % BANK, :]
                                else:
                                    act.wait_ge(unit_done, at(i, per, u0 + cc + 1))
                                    src = B[cc % BANK][:, 0:T]
                                if s.o + j - 1 > 0:
                                    act.wait_ge(prod_done, at(i, tiles, s.o + j - 1))
                                A(TMP[:, (s.o + j) % 2, 0:T], src, ACT.Silu).then_inc(first_done, 1)
                            else:
                                operand_hi(s.o + j, tiles, i, Z[:, bass.ds(i * tiles + j, 1), 0, 0:T], T)
                    run(act, s, body)
                elif s.kind == "down" or s.kind == "out":
                    def body(i, t0, tiles, mods, u0, per):
                        for cc in range(per):
                            split_hi(u0 + cc + LEAD, per, i, next_words(s, cc, per))
                            if mods:
                                mod_loads(s, cc, i)
                            if cc % PER_TILE[s.kind] == PER_TILE[s.kind] - 1:
                                n = t0 + cc // PER_TILE[s.kind]
                                square(s.h, s.sq, n, tiles, i, H[:, bass.ds(i * tiles + n, 1), 0:T], T)
                    run(act, s, body)
                elif s.kind == "k" or s.kind == "q":
                    scale = DK ** -0.5 if s.kind == "k" else 1.0
                    dst = KTT if s.kind == "k" else QTT
                    for cc in range(4):
                        split_hi(s.u + cc + LEAD, 0, 0)
                        if s.kind == "k" and cc == 0:
                            act.wait_ge(unit_done, s.u)
                            act.dma_start(CM[:], mix_in).then_inc(mixc_landed, 16)
                            y_hi(s)
                        if small:
                            half_copy(s, s.u + cc, 0, 0, cc, 0, s.o, 0)
                        else:
                            act.wait_ge(unit_done, s.u + cc + 1)
                            A(dst[:, cc, 0:T], B[cc][:, 0:T], ACT.Copy, scale=scale).then_inc(evac_done, 1)
                elif s.kind == "v":
                    act.wait_ge(mixc_landed, 16 * (s.layer + 1))
                    lgw = 2 * HEADS * s.layer
                    for cc in range(8):
                        split_hi(s.u + cc + LEAD, 0, 0)
                        if cc % 2 == 0:
                            h = cc // 2
                            f, b = LG[:, lgw + h:lgw + h + 1], LG[:, lgw + HEADS + h:lgw + HEADS + h + 1]
                            for n, (col, g) in enumerate(((CM_RELP, f), (CM_RELN, b), (CM_CF, f), (CM_CB, b))):
                                if h or s.layer:
                                    act.wait_ge(dec_done, 2 * (HEADS * s.layer + h) - (1 if n < 2 else 0))
                                A(G4[:, n, :], CM[:, col:col + 512], ACT.Exp, scale=g).then_inc(exp_done, 1)
                        if cc % 4 == 3:
                            act.wait_ge(unit_done, s.u + cc + 1)
                            for tt in range(4):
                                A(V[:, tt, (cc // 4) * 512:(cc // 4 + 1) * 512], B[tt][:], ACT.Copy
                                  ).then_inc(evac_done, 1)
                elif s.kind == "ret":
                    nO = 1 if small else 2

                    def head_out(h):
                        for e in range(nO):
                            act.wait_ge(ov_done, s.ov + nO * h + e + 1)
                            A(O[:, 2 * h:2 * h + 2, e * NX:(e + 1) * NX],
                              B[5 + e][:].rearrange("p (a b) -> p a b", a=2), ACT.Copy).then_inc(evac_done, 1)
                        act.wait_ge(evac_done, s.evac + nO * (h + 1))
                        if h >= 2:
                            act.wait_ge(ss_done, s.ss + h - 1)
                        A(TMP[:, 2 * (h % 2):2 * (h % 2) + 2, 0:T], O[:, 2 * h:2 * h + 2, 0:T], ACT.Square
                          ).then_inc(osq_done, 1)

                    def head_root(h):
                        if h:
                            act.wait_ge(on_done, s.on + 2 * h)
                        root(s.ss + h, DV, T, B[7])
                    head_out(0)
                    head_out(1)
                    head_root(0)
                    head_out(2)
                    head_root(1)
                    head_out(3)
                    head_root(2)
                    head_root(3)
                elif s.kind == "g":
                    def body(i, t0, tiles, mods, u0, per):
                        for cc in range(per):
                            if small:
                                half_copy(s, u0 + cc, per, i, cc, 0, s.o + cc - 1, per)
                            split_hi(u0 + cc + LEAD, per, i)
                            if small:
                                act.wait_ge(merged_done, at(i, per, s.merged + cc + 1))
                                src = HB[:, cc % BANK, :]
                            else:
                                act.wait_ge(unit_done, at(i, per, u0 + cc + 1))
                                src = B[cc % BANK][:, 0:T]
                            act.wait_ge(prod_done, at(i, per, s.o + cc - 1))
                            A(TMP[:, cc % 2, 0:T], src, ACT.Silu).then_inc(first_done, 1)
                            operand_hi(s.o + cc, per, i, R[:, bass.ds(i * per + cc, 1), 0, 0:T], T)
                    run(act, s, body)
                elif s.kind == "conv":
                    def body(i, t0, tiles, mods, u0, per):
                        for cc in range(per):
                            n, role = cc // 3, cc % 3
                            if small:
                                half_copy(s, u0 + cc, per, i, cc, 0, s.o + n, tiles)
                            split_hi(u0 + cc + LEAD, per, i)
                            if mods:
                                mod_loads(s, cc, i)
                            if role == 0 and not small:
                                act.wait_ge(unit_done, at(i, per, u0 + cc + 1))
                                act.wait_ge(prod_done, at(i, tiles, s.o + n - 1))
                                A(TMP[:, n % 2, 0:T], B[cc % BANK][:, 0:T], ACT.Copy).then_inc(first_done, 1)
                            if role == 2:
                                operand_hi(s.o + n, tiles, i, C[:, bass.ds(i * tiles + n, 1), 0, 0:T], T)
                    run(act, s, body)
                elif s.kind == "gates":
                    def body(i, t0, tiles, mods, u0, per):
                        for cc in range(per):
                            n, role = cc // 4, cc % 4
                            if small:
                                half_copy(s, u0 + cc, per, i, cc, 0, s.o + n, tiles)
                            split_hi(u0 + cc + LEAD, per, i)
                            if role < 2:
                                if small:
                                    act.wait_ge(merged_done, at(i, per, s.merged + cc + 1))
                                    src = HB[:, cc % BANK, :]
                                else:
                                    act.wait_ge(unit_done, at(i, per, u0 + cc + 1))
                                    src = B[cc % BANK][:, 0:T]
                                act.wait_ge(prod_done, at(i, tiles, s.o + n - (1 - role)))
                                dst = TMP[:, n % 2, 0:T] if role == 0 else CV[:, 0:T]
                                A(dst, src, ACT.Sigmoid).then_inc(first_done, 1)
                            if role == 3:
                                operand_hi(s.o + n, tiles, i, M[:, bass.ds(i * tiles + n, 1), 0, 0:T], T)
                    run(act, s, body)
                else:
                    root(s.ss, D, T, B[4])
                    for b in range(4):
                        act.wait_ge(out_turned, 8 + 8 * (b % 2))
                        t, kk = b // 2, b % 2
                        A(OROWS[:, t, kk * 512:(kk + 1) * 512], B[b][:], ACT.Copy).then_inc(out_copied, 1)

        @block.vector
        def _(dve):
            V_ = nc.vector

            def split_lo(u, per, i, words=UW):
                if u >= last_u and isinstance(i, int):
                    return
                dve.wait_ge(hi_done, at(i, per, u + 1))
                V_.tensor_tensor(LO[u % HL_SLOTS][:, 0:words], RAW[u % RAW_SLOTS][:, 0:words],
                                 HI[u % HL_SLOTS][:, 0:words].bitcast(F32), ALU.subtract).then_inc(lo_done, 1)

            def next_words(s, cc, per):
                return unit_words(s, cc + LEAD) if cc + LEAD < per else UW

            def mod_piece(sec, rate, i, k):
                dve.wait_ge(mod_landed[k % 2], at(i, 64 * rate, 16 * (4 * (sec - 2) + k // 2 + 1)))
                for cond in range(2):
                    acc, a = MODACC[:, cond, :], SC[:, cond, k:k + 1]
                    if k == 0:
                        V_.tensor_scalar(acc, MODRAW[0][:], a, None, ALU.mult).then_inc(mod_step, 1)
                    else:
                        dve.wait_ge(mod_step, at(i, 16 * rate, MOD0 + 16 * (sec - 2) + 2 * k + cond - 1))
                        V_.scalar_tensor_tensor(acc, MODRAW[k % 2][:], a, acc, ALU.mult, ALU.add
                                                ).then_inc(mod_step, 1)

            def mod_work(s, cc, per, i):
                if cc == 5:
                    mod_store(s.sec, 1, i)
                if cc < KT:
                    mod_piece(s.sec, 1, i, cc)
                if cc == KT + 1:
                    mod_reduce(s.sec, 1, i)

            def mod_reduce(sec, rate, i):
                dve.wait_ge(mod_step, at(i, 16 * rate, MOD0 + 16 * (sec - 1)))
                for r in range(4):
                    src = MODACC[:, r // 2, (r % 2) * 512:(r % 2 + 1) * 512]
                    if r:
                        dve.wait_ge(mod_fin, at(i, 8 * rate, 8 * (sec - 1) + 2 * r))
                    V_.transpose(MT[:], src).then_inc(mod_fin, 1)
                    dve.wait_ge(mod_fin, at(i, 8 * rate, 8 * (sec - 1) + 2 * r + 1))
                    V_.tensor_reduce(MR[:, 16 * r:16 * r + 16], MT[:].rearrange("p (b k) -> p b k", k=32),
                                     AXX, ALU.add).then_inc(mod_fin, 1)

            def bias_at(sec):
                return VT_BMOD[sec // SECTIONS] + sec % SECTIONS * KT

            def mod_store(sec, rate, i):
                dve.wait_ge(mod_sum, at(i, rate, sec - 1))
                total = B[5][:, 0:64].rearrange("p (c m r) -> p c m r", c=2, r=4)
                for r in range(4):
                    rows = slice(32 * r, 32 * r + 32)
                    for cond in range(2):
                        if rate:
                            dst = MODS[rows, bass.ds(i + sec, 1), cond, :]
                            bias = VT[rows, bass.ds(at(i, bias_at(sec) - bias_at(sec - 1), bias_at(sec - 1)), KT)]
                        else:
                            dst, bias = MODS[rows, sec, cond, :], VT[rows, bias_at(sec - 1):bias_at(sec - 1) + KT]
                        V_.tensor_tensor(dst, total[rows, cond, :, r], bias, ALU.add).then_inc(mods_ready, 1)

            def ready(sections):
                return 8 * (sections if sections <= 2 else sections + 1)

            def add_square(base, n, rate, i, T):
                dve.wait_ge(sq_done, at(i, rate, base - base // (KT + 1) + n + 1))
                dve.wait_ge(sqsum_done, at(i, rate, base + n + 1))
                V_.tensor_tensor(SQACC[:, 0:T], SQACC[:, 0:T], TMP[:, n % 2, 0:T], ALU.add).then_inc(sqsum_done, 1)

            def clear_squares():
                V_.memset(SQACC[:], 0.0).then_inc(sqsum_done, 1)

            def section(layer, n):
                sec = SECTIONS * layer + n
                return MODS[:, sec if sec < 2 else sec + 1, :, :]

            norm_count = [0]

            def reciprocal(ss, T):
                dve.wait_ge(rt_done, ss + 1)
                V_.reciprocal(RB[:, 0:T], RB[:, 0:T]).then_inc(rb_done, 1)
                dve.wait_ge(rb_done, ss + 1)

            def norm(s, which):
                T, layer = s.T, s.layer
                reciprocal(s.ss, T)
                dve.wait_ge(mods_ready, ready(SECTIONS * layer + 3 * which + 2))
                norm_count[0] += 1
                w = VT[:, VT_NORM + (3 * layer + which) * KT:VT_NORM + (3 * layer + which + 1) * KT]
                for cond in range(2):
                    V_.scalar_tensor_tensor(AMUL[:, cond, :], section(layer, 3 * which + 1)[:, cond, :], 1.0, w,
                                            ALU.add, ALU.mult).then_inc(amul_done, 1)
                dve.wait_ge(amul_done, 2 * norm_count[0])

                def scaled(k):
                    if k >= 4:
                        dve.wait_ge(ylo_done, s.y + k - 3)
                    V_.tensor_tensor(TMP[:, k % 4, 0:T], H[:, k, 0:T], RB[:, 0:T], ALU.mult).then_inc(y_scaled, 1)
                scaled(0)
                for k in range(KT):
                    if k + 1 < KT:
                        scaled(k + 1)
                    dve.wait_ge(y_scaled, s.y + k + 1)
                    for cond in range(T // NX):
                        t = TMP[:, k % 4, cond * NX:(cond + 1) * NX]
                        ins = V_.tensor_scalar(t, t, AMUL[:, cond, k:k + 1],
                                               section(layer, 3 * which)[:, cond, k:k + 1], ALU.mult, ALU.add)
                    ins.then_inc(y_done, 1)

            gate_count = [0]
            gate_set = sem("gate_set")

            def set_gate(s, sec, factor):
                dve.wait_ge(mods_ready, ready(SECTIONS * s.layer + sec + 1))
                gate_count[0] += 1
                V_.tensor_scalar(GATE[:], section(s.layer, sec), factor, None, ALU.mult).then_inc(gate_set, 1)
                dve.wait_ge(gate_set, gate_count[0])

            def residual(s, u, per, n, rate, i):
                dve.wait_ge(unit_done, at(i, per, u + 1))
                T = s.T
                for part in range(2):
                    cond = part if T == 512 else 0
                    cols = slice(cond * NX, (cond + 1) * NX)
                    dst = H[:, bass.ds(i * rate + n, 1), cols].rearrange("p a n -> p (a n)")
                    g = GATE[:, cond, bass.ds(i * rate + n, 1)]
                    if T == NX and part == 1:
                        dve.wait_ge(hpart_done, at(i, rate, s.hpart + n + 1))
                    ins = V_.scalar_tensor_tensor(dst, B[n % BANK][:, part * NX:(part + 1) * NX], g, dst,
                                                  ALU.mult, ALU.add)
                    ins.then_inc(hpart_done if part == 0 else h_done, 1)
            hpart_done = sem("hpart_done")
            def merge(s, c, rel, per, i, dst=None):
                dve.wait_ge(half_done, at(i, per, s.half + rel + 1))
                hb = HB[:, c % BANK, :]
                V_.tensor_tensor(dst if dst is not None else hb, B[c % BANK][:, 0:NX], hb, ALU.add
                                 ).then_inc(merged_done, 1)

            V_.memset(ONES[:], 1.0).then_inc(small_set, 1)
            V_.memset(EPST[:], EPS).then_inc(small_set, 1)
            V_.memset(U[:], 0.0).then_inc(small_set, 1)
            V_.memset(SCP[:].bitcast(F32), 0.0).then_inc(small_set, 1)
            V_.memset(MODACC[:], 0.0).then_inc(mod_step, MOD0)
            V_.memset(MR[:], 0.0).then_inc(mod_fin, 8)
            clear_squares()
            for g in range(3):
                n = P if g < 2 else KT
                dve.wait_ge(vec_turned, g + 1)
                V_.tensor_copy(VT[:, g * P:g * P + n], B[4 + g][:, 0:n]).then_inc(vt_done, 1)
            for cond in range(2):
                dve.wait_ge(scp_hi, cond + 1)
                ins = V_.tensor_tensor(SCP[:, :, 2 * cond + 1], SC[:, cond, :], SCP[:, :, 2 * cond].bitcast(F32),
                                       ALU.subtract)
            ins.then_inc(scp_lo, 1)
            for u in range(LEAD):
                split_lo(u, 0, 0)

            for s in stages:
                T, small = s.T, s.T == NX
                if s.kind == "ada":
                    for cc in range(2 * KT):
                        split_lo(s.u + cc + LEAD, 0, 0)
                        if cc in (6, 10):
                            k0 = 0 if cc == 6 else 4
                            for k in range(k0, k0 + 4):
                                dve.wait_ge(x_turned, k + 1)
                                V_.tensor_copy(H[:, k, :], B[4 + k % 4][:]).then_inc(h_done, 1)
                                if k > k0:
                                    add_square(0, k - 1, 0, 0, 512)
                            add_square(0, k0 + 3, 0, 0, 512)
                    dve.wait_ge(unit_done, s.u + 2 * KT)
                    for b in (0, 2):
                        V_.tensor_copy(ADAROWS[0:4, b * 512:(b + 1) * 512], B[b][0:4, :]).then_inc(ada_rows, 1)
                    dve.wait_ge(ada_turned, 1)
                    total = B[5][:, 0:4 * KT].rearrange("p (s m c) -> p s m c", s=2, c=2)
                    bias = VT[:, VT_BMOD[0]:VT_BMOD[0] + 2 * KT].rearrange("p (s m) -> p s m", s=2)
                    for cond in range(2):
                        V_.tensor_tensor(MODS[:, 0:2, cond, :], total[:, :, :, cond], bias, ALU.add
                                         ).then_inc(mods_ready, 8)
                elif s.kind == "up":
                    def body(i, t0, tiles, mods, u0, per):
                        for cc in range(per):
                            j, jj = t0 + cc // 2, cc // 2
                            o = s.o + j
                            if small and t0 + cc:
                                merge(s, cc, 2 * t0 + cc, per, i)
                            piece_first = mods and cc % 2 == 0 and cc > 0
                            if piece_first:
                                mod_work(s, cc, per, i)
                            split_lo(u0 + cc + LEAD, per, i)
                            if t0 == 0 and cc == 0:
                                norm(s, 2 * s.which)
                                if small:
                                    merge(s, 0, 0, per, i)
                            if mods and not piece_first:
                                mod_work(s, cc, per, i)
                            if cc % 2 == 1:
                                dve.wait_ge(first_done, at(i, tiles, s.first + j + 1))
                                if o - 1 > 0:
                                    dve.wait_ge(oplo_done, at(i, tiles, o - 1))
                                if small:
                                    dve.wait_ge(merged_done, at(i, per, s.merged + 2 * t0 + cc + 1))
                                    src = HB[:, cc % BANK, :]
                                else:
                                    dve.wait_ge(unit_done, at(i, per, u0 + cc + 1))
                                    src = B[cc % BANK][:, 0:T]
                                V_.tensor_tensor(TMP[:, 2 + o % 2, 0:T], src, TMP[:, o % 2, 0:T], ALU.mult
                                                 ).then_inc(prod_done, 1)
                        if mods:
                            mod_reduce(s.sec, 1, i)
                    run(dve, s, body)
                elif s.kind == "down" or s.kind == "out":
                    pt = PER_TILE[s.kind]
                    first = [True]

                    set_gate(s, 5 if s.kind == "out" else 6 * s.which + 2, 1.0 if s.kind == "out" else 0.5)
                    clear_squares()

                    def body(i, t0, tiles, mods, u0, per):
                        for cc in range(per):
                            split_lo(u0 + cc + LEAD, per, i, next_words(s, cc, per))
                            if mods:
                                mod_work(s, cc, per, i)
                            if cc % pt == pt - 1:
                                n = t0 + cc // pt
                                residual(s, u0 + cc, per, n, tiles, i)
                                add_square(s.sq, n, tiles, i, T)
                    run(dve, s, body)
                    if s.mods_end:
                        mod_store(DEPTH * SECTIONS, 0, 0)
                elif s.kind == "k" or s.kind == "q":
                    for cc in range(4):
                        split_lo(s.u + cc + LEAD, 0, 0)
                        if s.kind == "k" and cc == 0:
                            norm(s, 1)
                        if small:
                            merge(s, cc, cc, 0, 0, QTT[:, cc, 0:NX])
                elif s.kind == "v":
                    def heads2(ap):
                        return ap.rearrange("p (a n) -> p a n", a=1).broadcast_to([P, 2, NX])
                    cos, sin = heads2(CM[:, CM_COS:CM_COS + NX]), heads2(CM[:, CM_SIN:CM_SIN + NX])
                    dve.wait_ge(mixc_landed, 16 * (s.layer + 1))
                    for cc in range(8):
                        split_lo(s.u + cc + LEAD, 0, 0)
                        if cc % 2 == 1:
                            g = cc // 2
                            src = (KTT if g < 2 else QTT)[:, 2 * (g % 2):2 * (g % 2) + 2, 0:NX]
                            a = TMP[:, 0, :].rearrange("p (a n) -> p a n", a=2)
                            b = TMP[:, 1, :].rearrange("p (a n) -> p a n", a=2)
                            n = 4 * s.layer + g
                            if n > 0:
                                dve.wait_ge(rope_done, n)
                            dve.wait_ge(rot_done, n + 1)
                            dve.wait_ge(evac_done, s.evac)
                            V_.tensor_tensor(a, src, cos, ALU.mult).then_inc(rope_part, 1)
                            V_.tensor_tensor(b, B[4 + g][:].rearrange("p (a n) -> p a n", a=2), sin, ALU.mult
                                             ).then_inc(rope_part, 1)
                            dve.wait_ge(rope_part, 2 * n + 2)
                            V_.tensor_tensor(src, a, b, ALU.add).then_inc(rope_done, 1)
                        else:
                            h = cc // 2
                            e, dp = 4 * (HEADS * s.layer + h), 2 * (HEADS * s.layer + h)
                            for n, (g, op) in enumerate(((0, ALU.is_ge), (1, ALU.is_le))):
                                dve.wait_ge(exp_done, e + n + 1)
                                V_.scalar_tensor_tensor(G4[:, g, :], CM[:, CM_REL:CM_REL + 512], 0.0, G4[:, g, :],
                                                        op, ALU.mult).then_inc(dec_part, 1)
                            dve.wait_ge(dec_part, dp + 2)
                            V_.tensor_tensor(DEC[:, h, 0:2, :].rearrange("p a n -> p (a n)"), G4[:, 0, :], G4[:, 1, :],
                                             ALU.add).then_inc(dec_done, 1)
                            dve.wait_ge(exp_done, e + 4)
                            V_.tensor_tensor(DEC[:, h, 2:4, :].rearrange("p a n -> p (a n)"), G4[:, 2, :], G4[:, 3, :],
                                             ALU.add).then_inc(dec_done, 1)
                elif s.kind == "ret":
                    nP, nO = (2, 1) if small else (3, 2)
                    dve.wait_ge(dec_done, 2 * HEADS * (s.layer + 1))

                    def probs(h):
                        if h >= 2:
                            dve.wait_ge(ov_done, s.ov + nO * (h - 1))
                        for t in range(nP):
                            dve.wait_ge(score_done, s.score + nP * h + t + 1)
                            bank = B[2 * (h % 2) + t] if t < 2 else B[4]
                            dst = PX[:, h % 2, 2 * t:2 * t + 2, :] if t < 2 else PC[:, h % 2, :, :]
                            d = DEC[:, h, 2 * t:2 * t + 2, :] if t < 2 else DEC[:, h, 0:2, :]
                            V_.tensor_tensor(dst, bank[:].rearrange("p (a n) -> p a n", a=2), d, ALU.mult
                                             ).then_inc(mix_done, 1)

                    def head_norm(h):
                        reciprocal(s.ss + h, T)
                        for dv in range(2):
                            V_.tensor_tensor(O[:, 2 * h + dv, 0:T], O[:, 2 * h + dv, 0:T], RB[:, 0:T], ALU.mult
                                             ).then_inc(on_done, 1)

                    def head_sum(h):
                        dve.wait_ge(osq_done, HEADS * s.layer + h + 1)
                        t = TMP[:, 2 * (h % 2), 0:T]
                        V_.tensor_tensor(t, t, TMP[:, 2 * (h % 2) + 1, 0:T], ALU.add).then_inc(osum_done, 1)
                    probs(0)
                    probs(1)
                    probs(2)
                    head_sum(0)
                    probs(3)
                    head_sum(1)
                    head_norm(0)
                    head_sum(2)
                    head_norm(1)
                    head_sum(3)
                    head_norm(2)
                    head_norm(3)
                elif s.kind == "g":
                    def body(i, t0, tiles, mods, u0, per):
                        for cc in range(per):
                            o = s.o + cc
                            if small:
                                merge(s, cc, cc, per, i)
                            split_lo(u0 + cc + LEAD, per, i)
                            dve.wait_ge(first_done, at(i, per, s.first + cc + 1))
                            dve.wait_ge(oplo_done, at(i, per, o - 1))
                            dve.wait_ge(on_done, s.on)
                            V_.tensor_tensor(TMP[:, 2 + o % 2, 0:T], TMP[:, o % 2, 0:T],
                                             O[:, bass.ds(i * per + cc, 1), 0:T], ALU.mult).then_inc(prod_done, 1)
                    run(dve, s, body)
                elif s.kind == "conv":
                    segs = T // NX
                    dve.wait_ge(small_set, 3)

                    def body(i, t0, tiles, mods, u0, per):
                        for cc in range(per):
                            n, role = cc // 3, cc % 3
                            o = s.o + n
                            mx = s.mix + 4 * n
                            if small:
                                merge(s, cc, cc, per, i)
                            split_lo(u0 + cc + LEAD, per, i)
                            if mods:
                                mod_work(s, cc, per, i)
                            if role == 1:
                                if small:
                                    dve.wait_ge(merged_done, at(i, per, s.merged + cc + 1))
                                    a, b = HB[:, (cc - 1) % BANK, :], HB[:, cc % BANK, :]
                                else:
                                    dve.wait_ge(first_done, at(i, tiles, s.first + n + 1))
                                    dve.wait_ge(unit_done, at(i, per, u0 + cc + 1))
                                    a, b = TMP[:, n % 2, 0:T], B[cc % BANK][:, 0:T]
                                a, b = (v.rearrange("p (s n) -> p s n", s=segs) for v in (a, b))
                                dve.wait_ge(mix_done, at(i, 4 * tiles, mx))
                                dve.wait_ge(prod_done, at(i, tiles, o))
                                V_.tensor_tensor(U[:, 0:segs, 1:NX + 1], b, a, ALU.mult).then_inc(mix_done, 1)
                                acc = CV[:, 0:T].rearrange("p (s n) -> p s n", s=segs)
                                for tap in range(3):
                                    dve.wait_ge(mix_done, at(i, 4 * tiles, mx + 1 + tap))
                                    src = U[:, 0:segs, tap:tap + NX]
                                    wcol = VT_CONV + (3 * s.layer + tap) * KT + n
                                    w = VT[:, bass.ds(i * tiles + wcol, 1)]
                                    if tap == 0:
                                        V_.tensor_scalar(acc, src, w, None, ALU.mult).then_inc(mix_done, 1)
                                    else:
                                        V_.scalar_tensor_tensor(acc, src, w, acc, ALU.mult, ALU.add
                                                                ).then_inc(mix_done, 1)
                            if role == 2:
                                dve.wait_ge(mix_done, at(i, 4 * tiles, mx + 4))
                                dve.wait_ge(oplo_done, at(i, tiles, o - 1))
                                if small:
                                    dve.wait_ge(merged_done, at(i, per, s.merged + cc + 1))
                                    b = HB[:, cc % BANK, :]
                                else:
                                    dve.wait_ge(unit_done, at(i, per, u0 + cc + 1))
                                    b = B[cc % BANK][:, 0:T]
                                V_.tensor_tensor(TMP[:, 2 + o % 2, 0:T], b, CV[:, 0:T], ALU.mult
                                                 ).then_inc(prod_done, 1)
                    run(dve, s, body)
                elif s.kind == "gates":
                    def body(i, t0, tiles, mods, u0, per):
                        for cc in range(per):
                            n, role = cc // 4, cc % 4
                            o = s.o + n
                            if small:
                                merge(s, cc, cc, per, i)
                            split_lo(u0 + cc + LEAD, per, i)
                            if role < 2:
                                continue
                            if small:
                                dve.wait_ge(merged_done, at(i, per, s.merged + cc + 1))
                                b = HB[:, cc % BANK, :]
                            else:
                                dve.wait_ge(unit_done, at(i, per, u0 + cc + 1))
                                b = B[cc % BANK][:, 0:T]
                            dve.wait_ge(first_done, at(i, 2 * tiles, s.first + 2 * n + role - 1))
                            if role == 2:
                                dve.wait_ge(oplo_done, at(i, tiles, o - 1))
                                V_.tensor_tensor(TMP[:, 2 + o % 2, 0:T], b, TMP[:, o % 2, 0:T], ALU.mult
                                                 ).then_inc(mix_done, 1)
                            else:
                                V_.tensor_tensor(CV[:, 0:T], b, CV[:, 0:T], ALU.mult).then_inc(mix_done, 1)
                                dve.wait_ge(mix_done, at(i, 2 * tiles, s.mix + 2 * n + 2))
                                V_.tensor_tensor(TMP[:, 2 + o % 2, 0:T], TMP[:, 2 + o % 2, 0:T], CV[:, 0:T], ALU.add
                                                 ).then_inc(prod_done, 1)
                    run(dve, s, body)
                else:
                    reciprocal(s.ss, T)
                    for k in range(KT):
                        if k >= 4:
                            dve.wait_ge(out_turned, 2 * (k - 3))
                        V_.scalar_tensor_tensor(TMP[:, k % 4, 0:T], H[:, k, 0:T], VT[:, VT_FINAL + k:VT_FINAL + k + 1],
                                                RB[:, 0:T], ALU.mult, ALU.mult).then_inc(y_done, 1)

        @block.gpsimd
        def _(pool):
            def lo(dst, full, hi, s, count, rate, i, done):
                pool.wait_ge(s, at(i, rate, count))
                nc.gpsimd.tensor_tensor(dst, full, hi.bitcast(F32), ALU.subtract).then_inc(done, 1)

            def y_lo(s):
                for k in range(KT):
                    lo(Y[:, k, 1, 0:s.T], TMP[:, k % 4, 0:s.T], Y[:, k, 0, 0:s.T], yhi_done, s.y + k + 1, 0, 0, ylo_done)

            for s in stages:
                T = s.T
                if s.kind in ("up", "k"):
                    y_lo(s)
                if s.kind in ("up", "g", "conv", "gates"):
                    X = {"up": Z, "g": R, "conv": C, "gates": M}[s.kind]

                    def body(i, t0, tiles, mods, u0, per):
                        for n in range(tiles):
                            o = s.o + t0 + n
                            at = bass.ds(i * tiles + t0 + n, 1)
                            lo(X[:, at, 1, 0:T], TMP[:, 2 + o % 2, 0:T], X[:, at, 0, 0:T],
                               ophi_done, o + 1, tiles, i, oplo_done)
                    run(pool, s, body)


_INS = ["x", "c", "ctx", "c_ctx", "norm_w", "w_mod", "b_mod", "ffn1_w_up", "ffn1_w_down", "w_in",
        "ret_log_decay", "conv_w", "w_ret_out", "w_conv_out", "w_out", "ffn2_w_up", "ffn2_w_down",
        "final_norm_w"]


def kernel(**inputs):
    import concourse.bacc as bacc
    from concourse.bass_utils import run_bass_kernel_spmd

    nc = bacc.Bacc("TRN2", target_bir_lowering=False, num_devices=1, dynamic_dma_scratch_size=1024)
    arrays, args = {}, []
    tables = dict(zip(("keep", "mix"), constants()))
    for name in _INS + ["keep", "mix"]:
        a = np.ascontiguousarray(inputs[name] if name in inputs else tables[name])
        arrays[f"in_{name}_dram"] = a
        args.append(nc.dram_tensor(f"in_{name}_dram", a.shape, mybir.dt.from_np(a.dtype), kind="ExternalInput").ap())
    args.append(nc.dram_tensor("out_0_dram", (1, NX, D), F32, kind="ExternalOutput").ap())
    build(nc, *args)
    r = run_bass_kernel_spmd(nc, [arrays], core_ids=[0])
    return r.results[0]["out_0_dram"]
```
